# Optimizing a Trainium2 kernel written in Bass

```python
import math
import jax, jax.numpy as jnp
from jax import lax
import numpy as np

D_MODEL = 1024
BATCH = 1
SEQ = 256
DEPTH = 2

D_MIX = D_MODEL
HEAD_DIM = 64
M_WIDTH = D_MIX // 2
M_HEAD_DIM = 128
M_HEADS = M_WIDTH // M_HEAD_DIM
M_CHUNK = 64
CONV_W = 4
B_WIDTH = D_MIX // 4
B_HEADS = B_WIDTH // HEAD_DIM
MOBA_BLOCK = 256
MOBA_TOPK = 3
N_WIDTH = D_MIX // 4
N_HEADS = N_WIDTH // HEAD_DIM
CMP_LEN = 32
CMP_STRIDE = 16
CMP_HIDDEN = 128
SEL_BLOCK = 64
SEL_TOPK = 16
WINDOW = 512
Q_BLOCK = 64
D_FF = 4 * D_MODEL
ROPE_THETA = 500000.0
ROT_DIM = HEAD_DIM // 4
NORM_EPS = 1e-6
NEG = -1e30
BIG = 1e9

SPLITS = ((M_WIDTH,) * 4 + (M_HEADS, M_HEADS)
          + (B_WIDTH,) * 3
          + (N_WIDTH,) + (HEAD_DIM,) * 6
          + (3 * N_HEADS,))
D_IN = sum(SPLITS)
SPLIT_POINTS = tuple(int(v) for v in np.cumsum(SPLITS)[:-1])


def rmsnorm(x, g):
    xf = x.astype(jnp.float32)
    y = xf * lax.rsqrt(jnp.mean(xf * xf, axis=-1, keepdims=True) + NORM_EPS)
    return (y * g.astype(jnp.float32)).astype(x.dtype)

def partial_rope(x):
    S = x.shape[-2]
    half = ROT_DIM // 2
    inv_freq = jnp.exp(-math.log(ROPE_THETA) * jnp.arange(half, dtype=jnp.float32) * (2.0 / ROT_DIM))
    ang = jnp.arange(S, dtype=jnp.float32)[:, None] * inv_freq[None, :]
    cos, sin = jnp.cos(ang), jnp.sin(ang)
    x1, x2, rest = x[..., :half], x[..., half:ROT_DIM], x[..., ROT_DIM:]
    return jnp.concatenate([x1 * cos - x2 * sin, x2 * cos + x1 * sin, rest], axis=-1)

def causal_conv(x, w):
    S = x.shape[1]
    xp = jnp.pad(x, ((0, 0), (CONV_W - 1, 0), (0, 0)))
    return sum(xp[:, j:j + S] * w[j] for j in range(CONV_W))

def masked_softmax(s, mask):
    p = jax.nn.softmax(jnp.where(mask, s, NEG), axis=-1)
    return jnp.where(mask, p, 0.0)

def mlstm(q, k, v, o_pre, i_pre, f_pre, norm_g):
    B, S, _ = q.shape
    NC, L, H, D = S // M_CHUNK, M_CHUNK, M_HEADS, M_HEAD_DIM

    def to_chunks(t):
        return t.reshape(B, NC, L, H, D).transpose(1, 0, 3, 2, 4)

    qc, kc, vc = to_chunks(q), to_chunks(k) * (D ** -0.5), to_chunks(v)
    lf = jax.nn.log_sigmoid(f_pre).reshape(B, NC, L, H).transpose(1, 0, 3, 2)
    li = i_pre.reshape(B, NC, L, H).transpose(1, 0, 3, 2)
    causal = jnp.tril(jnp.ones((L, L), dtype=bool))

    def step(carry, xs):
        C, n, m = carry
        qt, kt, vt, lft, lit = xs
        b = jnp.cumsum(lft, axis=-1)
        dmat = jnp.where(causal, b[..., :, None] - b[..., None, :] + lit[..., None, :], -jnp.inf)
        inter = b + m[..., None]
        m_t = jnp.maximum(inter, jnp.max(dmat, axis=-1))
        w_intra = jnp.exp(dmat - m_t[..., None])
        w_prev = jnp.exp(inter - m_t)
        s = jnp.einsum('bhtd,bhsd->bhts', qt, kt) * w_intra
        num = jnp.einsum('bhts,bhse->bhte', s, vt) + w_prev[..., None] * jnp.einsum('bhtd,bhde->bhte', qt, C)
        den = jnp.sum(s, axis=-1) + w_prev * jnp.einsum('bhtd,bhd->bht', qt, n)
        h = num / jnp.maximum(jnp.abs(den), jnp.exp(-m_t))[..., None]
        b_last = b[..., -1]
        g = b_last[..., None] - b + lit
        m_new = jnp.maximum(b_last + m, jnp.max(g, axis=-1))
        a = jnp.exp(b_last + m - m_new)
        w_s = jnp.exp(g - m_new[..., None])
        C = a[..., None, None] * C + jnp.einsum('bhs,bhsd,bhse->bhde', w_s, kt, vt)
        n = a[..., None] * n + jnp.einsum('bhs,bhsd->bhd', w_s, kt)
        return (C, n, m_new), h

    init = (jnp.zeros((B, H, D, D), jnp.float32), jnp.zeros((B, H, D), jnp.float32),
            jnp.zeros((B, H), jnp.float32))
    _, h = lax.scan(step, init, (qc, kc, vc, lf, li))
    h = h.transpose(1, 0, 3, 2, 4).reshape(B, S, H, D)
    h = rmsnorm(h, norm_g.reshape(H, D)).reshape(B, S, M_WIDTH)
    return jax.nn.sigmoid(o_pre) * h

def moba(q, k, v, q_g, k_g):
    B, S, _ = q.shape
    H, D, BS = B_HEADS, HEAD_DIM, MOBA_BLOCK
    heads = lambda t: t.reshape(B, S, H, D).transpose(0, 2, 1, 3)
    q = partial_rope(rmsnorm(heads(q), q_g))
    k = partial_rope(rmsnorm(heads(k), k_g))
    v = heads(v)
    NB = -(-S // BS)
    pad = NB * BS - S
    kp = jnp.pad(k, ((0, 0), (0, 0), (0, pad), (0, 0)))
    vp = jnp.pad(v, ((0, 0), (0, 0), (0, pad), (0, 0)))
    kb = kp.reshape(B, H, NB, BS, D)
    vb = vp.reshape(B, H, NB, BS, D)
    kmean = jnp.mean(kb, axis=3)
    topk = min(MOBA_TOPK, NB)
    scale = D ** -0.5
    gather = jax.vmap(jax.vmap(lambda blocks, idx: blocks[idx]))

    def block(j):
        t0 = j * Q_BLOCK
        tq = t0 + jnp.arange(Q_BLOCK)
        qj = lax.dynamic_slice_in_dim(q, t0, Q_BLOCK, axis=2)
        own = t0 // BS
        gs = jnp.einsum('bhqd,bhnd->bhqn', qj, kmean)
        gs = jnp.where(jnp.arange(NB) < own, gs, NEG)
        _, idx = lax.top_k(gs, topk)
        gk, gv = gather(kb, idx), gather(vb, idx)
        s_sel = jnp.einsum('bhqd,bhqrkd->bhqrk', qj, gk) * scale
        s_sel = jnp.where((jnp.arange(topk) < own)[:, None], s_sel, NEG).reshape(B, H, Q_BLOCK, topk * BS)
        ko = lax.dynamic_slice_in_dim(kp, own * BS, BS, axis=2)
        vo = lax.dynamic_slice_in_dim(vp, own * BS, BS, axis=2)
        s_own = jnp.einsum('bhqd,bhkd->bhqk', qj, ko) * scale
        s_own = jnp.where(own * BS + jnp.arange(BS)[None, :] <= tq[:, None], s_own, NEG)
        p = jax.nn.softmax(jnp.concatenate([s_sel, s_own], axis=-1), axis=-1)
        p_sel = p[..., :topk * BS].reshape(B, H, Q_BLOCK, topk, BS)
        p_own = p[..., topk * BS:]
        return (jnp.einsum('bhqrk,bhqrkd->bhqd', p_sel, gv)
                + jnp.einsum('bhqk,bhkd->bhqd', p_own, vo))

    out = lax.map(block, jnp.arange(S // Q_BLOCK))
    return out.transpose(1, 0, 3, 2, 4).reshape(B, S, B_WIDTH)

def nsa(q, kc, vc, ks, vs, kw, vw, g_pre, q_g, k_g, pe, w1, w2):
    B, S, _ = q.shape
    H, D = N_HEADS, HEAD_DIM
    scale = D ** -0.5
    q = rmsnorm(q.reshape(B, S, H, D), q_g).transpose(0, 2, 1, 3)
    qr = partial_rope(q)
    ks = partial_rope(rmsnorm(ks, k_g[1]))
    kw = partial_rope(rmsnorm(kw, k_g[2]))

    n_sub = CMP_LEN // CMP_STRIDE
    Nc = S // CMP_STRIDE - n_sub + 1

    def compress(t, pe_, w1_, w2_):
        c = t.reshape(B, S // CMP_STRIDE, CMP_STRIDE, D)
        blocks = jnp.concatenate([c[:, r:Nc + r] for r in range(n_sub)], axis=2) + pe_
        hid = jax.nn.silu(blocks.reshape(B, Nc, CMP_LEN * D) @ w1_)
        return hid @ w2_

    Kc = rmsnorm(compress(kc, pe[0], w1[0], w2[0]), k_g[0])
    Vc = compress(vc, pe[1], w1[1], w2[1])
    c_end = jnp.arange(Nc) * CMP_STRIDE + CMP_LEN - 1

    Nsel = S // SEL_BLOCK
    c_start = np.arange(Nc) * CMP_STRIDE
    s_start = np.arange(Nsel) * SEL_BLOCK
    overlap = jnp.asarray(((c_start[:, None] < s_start[None, :] + SEL_BLOCK)
                           & (c_start[:, None] + CMP_LEN > s_start[None, :])).astype(np.float32))
    ksb = ks.reshape(B, Nsel, SEL_BLOCK, D)
    vsb = vs.reshape(B, Nsel, SEL_BLOCK, D)
    ksel = min(SEL_TOPK, Nsel)
    gather_b = jax.vmap(lambda blocks, idx: blocks[idx])
    kw_pad = jnp.pad(kw, ((0, 0), (WINDOW, 0), (0, 0)))
    vw_pad = jnp.pad(vw, ((0, 0), (WINDOW, 0), (0, 0)))
    gates = jax.nn.sigmoid(g_pre).reshape(B, S, 3, H)

    def block(j):
        t0 = j * Q_BLOCK
        tq = t0 + jnp.arange(Q_BLOCK)
        qj = lax.dynamic_slice_in_dim(q, t0, Q_BLOCK, axis=2)
        qrj = lax.dynamic_slice_in_dim(qr, t0, Q_BLOCK, axis=2)
        s_c = jnp.einsum('bhqd,bcd->bhqc', qj, Kc) * scale
        p_c = masked_softmax(s_c, c_end[None, :] <= tq[:, None])
        o_c = jnp.einsum('bhqc,bcd->bhqd', p_c, Vc)
        imp = jnp.einsum('bhqc,cn->bqn', p_c, overlap)
        blk_q = tq // SEL_BLOCK
        jn = jnp.arange(Nsel)
        causal_blk = jn[None, :] <= blk_q[:, None]
        forced = causal_blk & ((jn[None, :] == 0) | (jn[None, :] >= blk_q[:, None] - 1))
        imp = jnp.where(forced, BIG, jnp.where(causal_blk, imp, NEG))
        _, sidx = lax.top_k(imp, ksel)
        gk, gv = gather_b(ksb, sidx), gather_b(vsb, sidx)
        pos = sidx[..., None] * SEL_BLOCK + jnp.arange(SEL_BLOCK)
        mask_s = (pos <= tq[None, :, None, None])[:, None]
        s_s = jnp.where(mask_s, jnp.einsum('bhqd,bqrkd->bhqrk', qrj, gk) * scale, NEG)
        p_s = jax.nn.softmax(s_s.reshape(B, H, Q_BLOCK, ksel * SEL_BLOCK), axis=-1)
        o_s = jnp.einsum('bhqrk,bqrkd->bhqd', p_s.reshape(B, H, Q_BLOCK, ksel, SEL_BLOCK), gv)
        kwj = lax.dynamic_slice_in_dim(kw_pad, t0, WINDOW + Q_BLOCK, axis=1)
        vwj = lax.dynamic_slice_in_dim(vw_pad, t0, WINDOW + Q_BLOCK, axis=1)
        posw = t0 - WINDOW + jnp.arange(WINDOW + Q_BLOCK)
        mask_w = ((posw[None, :] <= tq[:, None]) & (posw[None, :] > tq[:, None] - WINDOW)
                  & (posw[None, :] >= 0))
        s_w = jnp.where(mask_w, jnp.einsum('bhqd,bkd->bhqk', qrj, kwj) * scale, NEG)
        o_w = jnp.einsum('bhqk,bkd->bhqd', jax.nn.softmax(s_w, axis=-1), vwj)
        gj = lax.dynamic_slice_in_dim(gates, t0, Q_BLOCK, axis=1).transpose(0, 2, 3, 1)[..., None]
        return gj[:, 0] * o_c + gj[:, 1] * o_s + gj[:, 2] * o_w

    out = lax.map(block, jnp.arange(S // Q_BLOCK))
    return out.transpose(1, 0, 3, 2, 4).reshape(B, S, N_WIDTH)

def first_inputs(seed: int = 0) -> dict:
    key = jax.random.key(seed)
    ks = jax.random.split(key, 20)
    nrm = lambda k, shape, s: jax.random.normal(k, shape, jnp.float32) * s
    L = DEPTH
    b_i = nrm(ks[2], (L, M_HEADS), 0.1)
    b_f = jnp.linspace(3.0, 6.0, M_HEADS, dtype=jnp.float32)[None, :] + nrm(ks[3], (L, M_HEADS), 0.1)
    return {
        "x": nrm(ks[0], (BATCH, SEQ, D_MODEL), 1.0),
        "w_in": nrm(ks[1], (L, D_MODEL, D_IN), D_MODEL ** -0.5),
        "b_if": jnp.concatenate([b_i, b_f], axis=-1),
        "conv_qk": nrm(ks[4], (L, CONV_W, 2 * M_WIDTH), CONV_W ** -0.5),
        "m_norm": 1.0 + nrm(ks[5], (L, M_WIDTH), 0.02),
        "moba_qk_norm": 1.0 + nrm(ks[6], (L, 2, HEAD_DIM), 0.02),
        "nsa_q_norm": 1.0 + nrm(ks[7], (L, HEAD_DIM), 0.02),
        "nsa_k_norm": 1.0 + nrm(ks[8], (L, 3, HEAD_DIM), 0.02),
        "cmp_pe": nrm(ks[9], (L, 2, CMP_LEN, HEAD_DIM), 0.02),
        "cmp_w1": nrm(ks[10], (L, 2, CMP_LEN * HEAD_DIM, CMP_HIDDEN), (CMP_LEN * HEAD_DIM) ** -0.5),
        "cmp_w2": nrm(ks[11], (L, 2, CMP_HIDDEN, HEAD_DIM), CMP_HIDDEN ** -0.5),
        "w_out": nrm(ks[12], (L, D_MIX, D_MODEL), D_MIX ** -0.5),
        "norm_mix": 1.0 + nrm(ks[13], (L, D_MODEL), 0.02),
        "norm_ffn": 1.0 + nrm(ks[14], (L, D_MODEL), 0.02),
        "w_ff1": nrm(ks[15], (L, D_MODEL, D_FF), D_MODEL ** -0.5),
        "w_ff2": nrm(ks[16], (L, D_FF, D_MODEL), D_FF ** -0.5),
    }

def first_block(x, w_in, b_if, conv_qk, m_norm, moba_qk_norm, nsa_q_norm, nsa_k_norm,
              cmp_pe, cmp_w1, cmp_w2, w_out, norm_mix, norm_ffn, w_ff1, w_ff2):
    for l in range(DEPTH):
        h = rmsnorm(x, norm_mix[l])
        proj = jnp.einsum('bsd,de->bse', h, w_in[l]).astype(jnp.float32)
        (m_q, m_k, m_v, m_o, m_i, m_f, b_q, b_k, b_v,
         n_q, n_kc, n_vc, n_ks, n_vs, n_kw, n_vw, n_g) = jnp.split(proj, SPLIT_POINTS, axis=-1)
        qk = jax.nn.silu(causal_conv(jnp.concatenate([m_q, m_k], axis=-1), conv_qk[l]))
        gif = jnp.concatenate([m_i, m_f], axis=-1) + b_if[l]
        y_m = mlstm(qk[..., :M_WIDTH], qk[..., M_WIDTH:], m_v, m_o,
                    gif[..., :M_HEADS], gif[..., M_HEADS:], m_norm[l])
        y_b = moba(b_q, b_k, b_v, moba_qk_norm[l, 0], moba_qk_norm[l, 1])
        y_n = nsa(n_q, n_kc, n_vc, n_ks, n_vs, n_kw, n_vw, n_g, nsa_q_norm[l], nsa_k_norm[l],
                  cmp_pe[l], cmp_w1[l], cmp_w2[l])
        mix = jnp.concatenate([y_m, y_b, y_n], axis=-1).astype(x.dtype)
        x = x + jnp.einsum('bse,ed->bsd', mix, w_out[l])
        h = rmsnorm(x, norm_ffn[l])
        u = jnp.square(jax.nn.relu(jnp.einsum('bsd,df->bsf', h, w_ff1[l])))
        x = x + jnp.einsum('bsf,fd->bsd', u, w_ff2[l])
    return x


GRID_W = 64
CTX_LEN = 256
N_MIXERS = 2
N_HEADS_2 = 8
N_KV_HEADS = 2
HEAD_DIM_2 = D_MODEL // N_HEADS_2
KV_REP = N_HEADS_2 // N_KV_HEADS
QKV_DIM = (N_HEADS_2 + 2 * N_KV_HEADS) * HEAD_DIM_2
Q_BLOCK_2 = 128
WINDOW_2 = 128
ROPE_THETA_2 = 10000.0
RMS_EPS = 1e-6
NEG_INF = -1e30
N_WINDOW_LAYERS = DEPTH // N_MIXERS
PEER_HEADS = 8
PEER_TOPK = 16
N_KEYS = 128
N_EXPERTS = N_KEYS * N_KEYS
PEER_QDIM = 256
PEER_BLOCK = 128
N_MOD = 6


def rms_norm(x, gain):
    xf = x.astype(jnp.float32)
    y = xf * lax.rsqrt(jnp.mean(xf * xf, axis=-1, keepdims=True) + RMS_EPS)
    return (y * gain.astype(jnp.float32)).astype(x.dtype)

def axial_rope_tables(n_tokens, dtype):
    rows = n_tokens // GRID_W
    row = jnp.repeat(jnp.arange(rows), GRID_W).astype(jnp.float32)
    col = jnp.tile(jnp.arange(GRID_W), rows).astype(jnp.float32)
    half = HEAD_DIM_2 // 2
    inv = ROPE_THETA_2 ** (-jnp.arange(0, half, 2, dtype=jnp.float32) / half)
    ang = jnp.concatenate([row[:, None] * inv, col[:, None] * inv], axis=-1)
    return jnp.cos(ang).astype(dtype), jnp.sin(ang).astype(dtype)

def apply_axial_rope(x, cos, sin):
    n = x.shape[1]
    xr = x.reshape(x.shape[:-1] + (2, 2, HEAD_DIM_2 // 4))
    x1 = xr[..., 0, :]
    x2 = xr[..., 1, :]
    c = cos.reshape(n, 1, 2, HEAD_DIM_2 // 4)
    s = sin.reshape(n, 1, 2, HEAD_DIM_2 // 4)
    out = jnp.stack([x1 * c - x2 * s, x1 * s + x2 * c], axis=-2)
    return out.reshape(x.shape)

def modulate(h, shift, scale):
    return h * (1 + scale) + shift

def project_qkv(h, w_qkv, q_gain, k_gain, rope):
    b, n, _ = h.shape
    y = h @ w_qkv
    q = y[..., : N_HEADS_2 * HEAD_DIM_2].reshape(b, n, N_HEADS_2, HEAD_DIM_2)
    k = y[..., N_HEADS_2 * HEAD_DIM_2:(N_HEADS_2 + N_KV_HEADS) * HEAD_DIM_2].reshape(b, n, N_KV_HEADS, HEAD_DIM_2)
    v = y[..., (N_HEADS_2 + N_KV_HEADS) * HEAD_DIM_2:].reshape(b, n, N_KV_HEADS, HEAD_DIM_2)
    q = rms_norm(q, q_gain)
    k = rms_norm(k, k_gain)
    if rope is not None:
        cos, sin = rope
        q = apply_axial_rope(q, cos, sin)
        k = apply_axial_rope(k, cos, sin)
    q = q.reshape(b, n, N_KV_HEADS, KV_REP, HEAD_DIM_2)
    return q, k, v

def latent_global_attention(q, k, v, kc, vc):
    b, n = q.shape[:2]
    nblk = n // Q_BLOCK_2
    scale = HEAD_DIM_2 ** -0.5
    ka = jnp.concatenate([kc, k], axis=1)
    va = jnp.concatenate([vc, v], axis=1)
    qb = jnp.moveaxis(q.reshape(b, nblk, Q_BLOCK_2, N_KV_HEADS, KV_REP, HEAD_DIM_2), 1, 0)

    def attend_block(qblk):
        s = jnp.einsum('bqgrd,bkgd->bgrqk', qblk, ka).astype(jnp.float32) * scale
        p = jax.nn.softmax(s, axis=-1)
        return jnp.einsum('bgrqk,bkgd->bqgrd', p.astype(va.dtype), va)

    o = lax.map(attend_block, qb)
    return jnp.moveaxis(o, 0, 1).reshape(b, n, N_HEADS_2 * HEAD_DIM_2)

def latent_window_attention(q, k, v, kc, vc, sink):
    b, n = q.shape[:2]
    nblk = n // Q_BLOCK_2
    span = Q_BLOCK_2 + 2 * WINDOW_2
    scale = HEAD_DIM_2 ** -0.5
    kp = jnp.pad(k, ((0, 0), (WINDOW_2, WINDOW_2), (0, 0), (0, 0)))
    vp = jnp.pad(v, ((0, 0), (WINDOW_2, WINDOW_2), (0, 0), (0, 0)))
    idx = jnp.arange(nblk)[:, None] * Q_BLOCK_2 + jnp.arange(span)[None, :]
    kb = kp[:, idx]
    vb = vp[:, idx]
    kpos = idx - WINDOW_2
    qpos = jnp.arange(nblk)[:, None] * Q_BLOCK_2 + jnp.arange(Q_BLOCK_2)[None, :]
    mask = ((kpos[:, None, :] >= 0) & (kpos[:, None, :] < n)
            & (jnp.abs(qpos[:, :, None] - kpos[:, None, :]) <= WINDOW_2))
    qb = q.reshape(b, nblk, Q_BLOCK_2, N_KV_HEADS, KV_REP, HEAD_DIM_2)
    s_loc = jnp.einsum('bnqgrd,bnkgd->bngrqk', qb, kb).astype(jnp.float32) * scale
    s_loc = jnp.where(mask[None, :, None, None], s_loc, NEG_INF)
    s_ctx = jnp.einsum('bnqgrd,bcgd->bngrqc', qb, kc).astype(jnp.float32) * scale
    sk = jnp.broadcast_to(sink.astype(jnp.float32).reshape(N_KV_HEADS, KV_REP, 1, 1),
                          s_loc.shape[:-1] + (1,))
    p = jax.nn.softmax(jnp.concatenate([s_loc, s_ctx, sk], axis=-1), axis=-1)
    p_loc = p[..., :span]
    p_ctx = p[..., span:span + kc.shape[1]]
    o = (jnp.einsum('bngrqk,bnkgd->bnqgrd', p_loc.astype(vb.dtype), vb)
         + jnp.einsum('bngrqc,bcgd->bnqgrd', p_ctx.astype(vc.dtype), vc))
    return o.reshape(b, n, N_HEADS_2 * HEAD_DIM_2)

def context_attention(qc, kc, vc, sink):
    b, n = qc.shape[:2]
    scale = HEAD_DIM_2 ** -0.5
    s = jnp.einsum('bqgrd,bkgd->bgrqk', qc, kc).astype(jnp.float32) * scale
    if sink is not None:
        sk = jnp.broadcast_to(sink.astype(jnp.float32).reshape(N_KV_HEADS, KV_REP, 1, 1),
                              s.shape[:-1] + (1,))
        p = jax.nn.softmax(jnp.concatenate([s, sk], axis=-1), axis=-1)[..., :n]
    else:
        p = jax.nn.softmax(s, axis=-1)
    o = jnp.einsum('bgrqk,bkgd->bqgrd', p.astype(vc.dtype), vc)
    return o.reshape(b, n, N_HEADS_2 * HEAD_DIM_2)

def peer_block(hb, w_q, sub_keys, u_tab, v_tab):
    n = hb.shape[0]
    q = (hb @ w_q).reshape(n, PEER_HEADS, PEER_QDIM)
    q1 = q[..., : PEER_QDIM // 2]
    q2 = q[..., PEER_QDIM // 2:]
    s1 = jnp.einsum('nhd,kd->nhk', q1, sub_keys[0]).astype(jnp.float32)
    s2 = jnp.einsum('nhd,kd->nhk', q2, sub_keys[1]).astype(jnp.float32)
    v1, i1 = lax.top_k(s1, PEER_TOPK)
    v2, i2 = lax.top_k(s2, PEER_TOPK)
    cand_s = (v1[..., :, None] + v2[..., None, :]).reshape(n, PEER_HEADS, PEER_TOPK * PEER_TOPK)
    cand_i = (i1[..., :, None] * N_KEYS + i2[..., None, :]).reshape(n, PEER_HEADS, PEER_TOPK * PEER_TOPK)
    top_s, pos = lax.top_k(cand_s, PEER_TOPK)
    expert = jnp.take_along_axis(cand_i, pos, axis=-1)
    g = jax.nn.softmax(top_s, axis=-1)
    u = u_tab[expert]
    act = jax.nn.gelu(jnp.einsum('nhkd,nd->nhk', u, hb).astype(jnp.float32))
    w = (g * act).astype(hb.dtype)
    return jnp.einsum('nhk,nhkd->nd', w, v_tab[expert])

def peer_ffn(h, w_q, sub_keys, u_tab, v_tab):
    b, n, d = h.shape
    hb = h.reshape(-1, PEER_BLOCK, d)
    out = lax.map(lambda blk: peer_block(blk, w_q, sub_keys, u_tab, v_tab), hb)
    return out.reshape(b, n, d)

def second_inputs(seed: int = 0) -> dict:
    key = jax.random.key(seed)
    ks = jax.random.split(key, 18)
    f32 = jnp.float32
    x = jax.random.normal(ks[0], (BATCH, SEQ, D_MODEL), f32)
    c = jax.random.normal(ks[1], (BATCH, D_MODEL), f32)
    ctx = jax.random.normal(ks[2], (BATCH, CTX_LEN, D_MODEL), f32)
    c_ctx = jax.random.normal(ks[3], (D_MODEL,), f32)
    ada_w = jax.random.normal(ks[4], (DEPTH, D_MODEL, N_MOD * D_MODEL), f32) * (0.5 * D_MODEL ** -0.5)
    ada_b = jax.random.normal(ks[5], (DEPTH, N_MOD * D_MODEL), f32) * 0.1
    norm1_gain = 1.0 + 0.02 * jax.random.normal(ks[6], (DEPTH, D_MODEL), f32)
    norm2_gain = 1.0 + 0.02 * jax.random.normal(ks[7], (DEPTH, D_MODEL), f32)
    w_qkv = jax.random.normal(ks[8], (DEPTH, D_MODEL, QKV_DIM), f32) * D_MODEL ** -0.5
    q_norm_gain = 1.0 + 0.02 * jax.random.normal(ks[9], (DEPTH, HEAD_DIM_2), f32)
    k_norm_gain = 1.0 + 0.02 * jax.random.normal(ks[10], (DEPTH, HEAD_DIM_2), f32)
    w_o = jax.random.normal(ks[11], (DEPTH, N_HEADS_2 * HEAD_DIM_2, D_MODEL), f32) * (N_HEADS_2 * HEAD_DIM_2) ** -0.5
    attn_sinks = jax.random.normal(ks[12], (N_WINDOW_LAYERS, N_HEADS_2), f32) * 0.5
    peer_w_q = jax.random.normal(ks[13], (DEPTH, D_MODEL, PEER_HEADS * PEER_QDIM), f32) * D_MODEL ** -0.5
    peer_sub_keys = jax.random.normal(ks[14], (DEPTH, 2, N_KEYS, PEER_QDIM // 2), f32) * (PEER_QDIM // 2) ** -0.5
    peer_u = jax.random.normal(ks[15], (DEPTH, N_EXPERTS, D_MODEL), f32) * D_MODEL ** -0.5
    peer_v = jax.random.normal(ks[16], (DEPTH, N_EXPERTS, D_MODEL), f32) * PEER_HEADS ** -0.5
    return {"x": x, "c": c, "ctx": ctx, "c_ctx": c_ctx, "ada_w": ada_w, "ada_b": ada_b,
            "norm1_gain": norm1_gain, "norm2_gain": norm2_gain, "w_qkv": w_qkv,
            "q_norm_gain": q_norm_gain, "k_norm_gain": k_norm_gain, "w_o": w_o,
            "attn_sinks": attn_sinks, "peer_w_q": peer_w_q, "peer_sub_keys": peer_sub_keys,
            "peer_u": peer_u, "peer_v": peer_v}

def second_block(x, c, ctx, c_ctx, ada_w, ada_b, norm1_gain, norm2_gain, w_qkv, q_norm_gain,
              k_norm_gain, w_o, attn_sinks, peer_w_q, peer_sub_keys, peer_u, peer_v):
    n_lat = x.shape[1]
    rope = axial_rope_tables(n_lat, x.dtype)
    xc = ctx
    for i in range(DEPTH):
        last = i == DEPTH - 1
        mod = jax.nn.silu(c) @ ada_w[i] + ada_b[i]
        sh1, sc1, g1, sh2, sc2, g2 = [m[:, None, :] for m in jnp.split(mod, N_MOD, axis=-1)]
        modc = jax.nn.silu(c_ctx) @ ada_w[i] + ada_b[i]
        csh1, csc1, cg1, csh2, csc2, cg2 = jnp.split(modc, N_MOD, axis=-1)

        h = modulate(rms_norm(x, norm1_gain[i]), sh1, sc1)
        hc = modulate(rms_norm(xc, norm1_gain[i]), csh1, csc1)
        q, k, v = project_qkv(h, w_qkv[i], q_norm_gain[i], k_norm_gain[i], rope)
        qc, kc, vc = project_qkv(hc, w_qkv[i], q_norm_gain[i], k_norm_gain[i], None)
        if i % N_MIXERS == 0:
            o = latent_global_attention(q, k, v, kc, vc)
            sink = None
        else:
            sink = attn_sinks[i // N_MIXERS]
            o = latent_window_attention(q, k, v, kc, vc, sink)
        x = x + g1 * (o @ w_o[i])
        if not last:
            oc = context_attention(qc, kc, vc, sink)
            xc = xc + cg1 * (oc @ w_o[i])

        h2 = modulate(rms_norm(x, norm2_gain[i]), sh2, sc2)
        x = x + g2 * peer_ffn(h2, peer_w_q[i], peer_sub_keys[i], peer_u[i], peer_v[i])
        if not last:
            h2c = modulate(rms_norm(xc, norm2_gain[i]), csh2, csc2)
            xc = xc + cg2 * peer_ffn(h2c, peer_w_q[i], peer_sub_keys[i], peer_u[i], peer_v[i])
    return x


def setup_inputs(seed=0):
    out = dict(first_inputs(seed))
    for name, value in second_inputs(seed + 1).items():
        if name != "x":
            out[name + "_2"] = value
    return out


def reference(
    x, w_in, b_if, conv_qk, m_norm, moba_qk_norm, nsa_q_norm, nsa_k_norm, cmp_pe, cmp_w1,
    cmp_w2, w_out, norm_mix, norm_ffn, w_ff1, w_ff2, c_2, ctx_2, c_ctx_2, ada_w_2, ada_b_2,
    norm1_gain_2, norm2_gain_2, w_qkv_2, q_norm_gain_2, k_norm_gain_2, w_o_2, attn_sinks_2,
    peer_w_q_2, peer_sub_keys_2, peer_u_2, peer_v_2,
):
    x = first_block(
        x, w_in, b_if, conv_qk, m_norm, moba_qk_norm, nsa_q_norm, nsa_k_norm, cmp_pe, cmp_w1,
        cmp_w2, w_out, norm_mix, norm_ffn, w_ff1, w_ff2,
    )
    return second_block(
        x, c_2, ctx_2, c_ctx_2, ada_w_2, ada_b_2, norm1_gain_2, norm2_gain_2, w_qkv_2,
        q_norm_gain_2, k_norm_gain_2, w_o_2, attn_sinks_2, peer_w_q_2, peer_sub_keys_2,
        peer_u_2, peer_v_2,
    )


_drawn_inputs = setup_inputs


def setup_inputs(seed=0):
    import zlib

    import numpy as np

    out = dict(_drawn_inputs(seed))
    spreads = {}
    factors = {'m_norm': 5.06,
     'moba_qk_norm': 8.0,
     'nsa_q_norm': 8.0,
     'nsa_k_norm': 8.0,
     'cmp_pe': 8.0,
     'norm_mix': 3.067,
     'ctx_2': 4.45,
     'norm1_gain_2': 8.0,
     'norm2_gain_2': 8.0,
     'q_norm_gain_2': 8.0,
     'k_norm_gain_2': 8.0,
     'attn_sinks_2': 8.0}
    for name, (base, spread) in spreads.items():
        noise = np.random.default_rng([zlib.crc32(name.encode()), seed]).standard_normal(out[name].shape)
        drawn = base * np.exp(spread * noise) if base else spread * noise
        out[name] = __import__('jax').numpy.asarray(drawn.astype(out[name].dtype))
    for name, factor in factors.items():
        out[name] = (out[name] * factor).astype(out[name].dtype)
    return out
```

```python
from contextlib import ExitStack

import numpy as np

import concourse.bass as bass
from concourse import mybir

P = 128
F32 = mybir.dt.float32
U32 = mybir.dt.uint32
ALU = mybir.AluOpType
ACT = mybir.ActivationFunctionType
AX = mybir.AxisListType.X

D = 1024
KT = D // P
S = 256
NT = S // P
DEPTH = 2
EPS = 1e-6
NEG = -1e30
EXP_MAX = 80.0

MW, MH, MD = 512, 4, 128
HD = 64
NG = 22
IF0 = 4 * MW
NAT0 = IF0 + 2 * MH
NAT = NG * HD + 12
D_IN = NAT0 + NAT
D_FF = 4 * D
NC_CMP = S // 16 - 1
CMP_H = 128

H2, KV2, HD2 = 8, 2, 128
N_MOD = 6
PH, TOPK, NK = 8, 16, 128
NE = NK * NK
GELU_C = 2.0 * float(np.sqrt(2.0 / np.pi))

CONST_COLS = {}


def constant_table():
    parts = {}
    i = np.arange(P)
    parts["ident"] = np.eye(P)
    parts["caus"] = np.concatenate([np.zeros((P, P)), np.where(i[None, :] <= i[:, None], 0.0, NEG)], 1)
    parts["causT"] = np.where(i[:, None] <= i[None, :], 0.0, NEG)
    tq = np.arange(S).reshape(NT, P).T[:, :, None]
    seen = (np.arange(NC_CMP) * 16 + 31)[None, None, :] <= tq
    parts["cmp_add"] = np.where(seen, 0.0, NEG).reshape(P, -1)
    parts["cmp_on"] = np.where(seen, 1.0, 0.0).reshape(P, -1)
    pos = np.arange(S, dtype=np.float32)
    inv = np.exp(np.float32(-np.log(500000.0)) * np.arange(8, dtype=np.float32) * np.float32(2.0 / 16)).astype(np.float32)
    ang = (pos[:, None] * inv[None, :]).astype(np.float32)
    per_tile = lambda a: a.reshape(NT, P, -1).transpose(1, 0, 2).reshape(P, -1)
    parts["cos1"], parts["sin1"] = per_tile(np.cos(ang)), per_tile(np.sin(ang))
    half = HD2 // 2
    inv2 = (np.float32(10000.0) ** (-np.arange(0, half, 2, dtype=np.float32) / np.float32(half))).astype(np.float32)
    row = np.repeat(np.arange(S // 64), 64).astype(np.float32)
    col = np.tile(np.arange(64), S // 64).astype(np.float32)
    ang2 = np.concatenate([row[:, None] * inv2, col[:, None] * inv2], 1).astype(np.float32)
    parts["cos2"], parts["sin2"] = per_tile(np.cos(ang2)), per_tile(np.sin(ang2))
    near = np.abs(pos[:, None] - pos[None, :]) <= 128
    win = np.concatenate([np.where(near, 0.0, NEG), np.zeros((S, S))], 1)
    parts["win"] = per_tile(win)
    parts["iota"] = np.tile(np.arange(TOPK), (P, 1))
    sel = np.zeros((P, 4, P))
    for h in range(4):
        sel[h, h] = 1.0
    parts["sel"] = sel.reshape(P, -1)
    parts["ones"] = np.ones((P, S))
    parts["m05"] = np.full((P, 48), -0.5)
    at = 0
    for name, a in parts.items():
        CONST_COLS[name] = (at, a.shape[1])
        at += a.shape[1]
    return np.concatenate(list(parts.values()), 1).astype(np.float32)


CONSTS = constant_table()


class Lane:

    def __init__(self, sem):
        self.sem, self.n, self.steps, self.seen = sem, 0, [], {}

    def waits(self, after):
        need = {}
        todo = list(after)
        while todo:
            a = todo.pop()
            if a is None:
                continue
            if isinstance(a, list):
                todo += a
                continue
            sem, v = a
            key = id(sem)
            if self.seen.get(key, 0) < v and (key not in need or need[key][1] < v):
                need[key] = (sem, v)
        for key, (_, v) in need.items():
            self.seen[key] = v
        return list(need.values())

    def do(self, fn, *after):
        self.n += 1
        self.steps.append((fn, self.waits(after), self.sem, 1))
        return (self.sem, self.n)

    def dma(self, count, out, in_, *after, scattered=False):
        count.n += 16
        self.steps.append((lambda e: e.dma_start(out, in_, allow_slow_non_contiguous=scattered), self.waits(after), count.sem, 16))
        return (count.sem, count.n)

    def play(self, e):
        for fn, waits, sem, by in self.steps:
            for s, v in waits:
                e.wait_ge(s, v)
            fn(e).then_inc(sem, by)


class Count:
    def __init__(self, sem):
        self.sem, self.n = sem, 0


class Turns:

    def __init__(self, bufs):
        self.bufs, self.free, self.i = bufs, [[] for _ in bufs], 0

    def take(self):
        i = self.i % len(self.bufs)
        self.i += 1
        free, self.free[i] = self.free[i], None
        assert free is not None, "a buffer is taken before its last reader is known"
        return i, self.bufs[i], free

    def done(self, i, *counts):
        self.free[i] = list(counts)


class Stage:
    def __init__(self, nc, sems, psum):
        self.nc, self.sems, self.used = nc, sems, 0
        self.pe, self.dve, self.act = Lane(self.sem()), Lane(self.sem()), Lane(self.sem())
        self.pool, self.sp = Lane(self.sem()), Lane(self.sem())
        self.soft = []
        self.ps = Turns([psum[:, 2 * i:2 * i + 2, :] for i in range(4)])

    def sem(self):
        self.used += 1
        return self.sems[self.used - 1]

    def count(self):
        return Count(self.sem())

    def play_pool(self, e):
        self.pool.play(e)
        if self.soft:
            for c in self.soft:
                e.wait_ge(c.sem, c.n)
            e.dma_reset()

    def run(self):
        with self.nc.Block() as block:
            block.sync(lambda e: self.sp.play(e))
            block.scalar(lambda e: self.act.play(e))
            block.vector(lambda e: self.dve.play(e))
            block.gpsimd(self.play_pool)
            block.tensor(lambda e: self.pe.play(e))
        self.nc.all_engine_barrier(sems_to_clear=range(self.sems[0].num, self.sems[self.used - 1].num + 1))


class Stream:

    def __init__(self, st, ring, plan):
        self.st, self.ring, self.plan = st, ring, plan
        self.counts = [st.count() for _ in ring]
        self.short = st.count()
        if any(len(p) > 2 for p in plan):
            st.soft.append(self.short)
        self.loaded, self.asked, self.at = [], 0, 0
        for _ in ring:
            self.load()

    def load(self, *after):
        if self.asked < len(self.plan):
            i = self.asked % len(self.ring)
            view, *parts = self.plan[self.asked]
            dst = view(self.ring[i])
            if len(parts) == 1:
                landed = self.st.sp.dma(self.counts[i], dst, parts[0], *after)
            else:
                for j, src in enumerate(parts):
                    landed = self.st.pool.dma(self.short, dst[:, j], src, *after)
            self.loaded.append((dst, landed))
            self.asked += 1

    def take(self):
        self.at += 1
        return self.loaded[self.at - 1]

    def done(self, *counts):
        self.load(*counts)


def mm_group(pairs):
    def fn(e):
        last = None
        for out, terms in pairs:
            for i, (a, b) in enumerate(terms):
                last = e.matmul(out, a, b, start=(i == 0), stop=(i == len(terms) - 1))
        return last
    return fn


def turned(items, ident):
    def fn(e):
        last = None
        for out, a in items:
            last = e.transpose(out, a, ident[0:a.shape[0], 0:a.shape[0]])
        return last
    return fn


def ts(out, a, s1, s2, op0, op1=None):
    if op1 is None:
        return lambda e: e.tensor_scalar(out, a, s1, None, op0)
    return lambda e: e.tensor_scalar(out, a, s1, s2, op0, op1)


def tt(out, a, b, op):
    return lambda e: e.tensor_tensor(out, a, b, op)


def stt(out, a, s, b, op0, op1):
    return lambda e: e.scalar_tensor_tensor(out=out, in0=a, scalar=s, in1=b, op0=op0, op1=op1)


def red(out, a, op, negate=False):
    if negate:
        return lambda e: e.tensor_reduce(out, a, AX, op, negate=True)
    return lambda e: e.tensor_reduce(out, a, AX, op)


def cp(out, a):
    return lambda e: e.tensor_copy(out, a)


def af(out, a, func, bias=None, scale=1.0, acc=None):
    def fn(e):
        kw = {} if acc is None else {"accum_out": acc}
        if bias is not None:
            kw["bias"] = bias
        return e.activation(out, a, func, scale=scale, **kw)
    return fn


def flat(ap, pattern, **kw):
    return ap.rearrange(pattern, **kw)


def wide(ap, shape, *axes):
    for a in axes:
        ap = ap.unsqueeze(a)
    return ap.to_broadcast(shape)


class Memory:
    def __init__(self, nc, ctx):
        self.nc, self.ctx = nc, ctx

    def __call__(self, name, shape, dt=F32):
        return self.ctx.enter_context(self.nc.sbuf_tensor(f"sb_{name}", shape, dt))


def rms_scale(st, out, ss, width, n, m05, *after):
    a = st.dve.do(ts(out, ss, 1.0 / width, EPS, ALU.mult, ALU.add), *after)
    return st.pool.do(tt(out, out, m05, ALU.pow), a)


def sigmoid_of(st, out, a, *after):
    t = st.dve.do(ts(out, a, -EXP_MAX, None, ALU.max), *after)
    t = st.act.do(af(out, out, ACT.Exp, scale=-1.0), t)
    t = st.dve.do(ts(out, out, 1.0, None, ALU.add), t)
    return st.dve.do(lambda e: e.reciprocal(out, out), t)


def first_block(st, sb, A, C, x, ring, l):
    pe, dve, act, pool, sp = st.pe, st.dve, st.act, st.pool, st.sp
    at = lambda name: A[name][bass.DynSlice(l, 1)]
    ident = C("ident")
    chunk = lambda w, c0, n: (lambda slot: slot[:, 0:KT * n].rearrange("p (k n) -> p k n", k=KT),
                              w.rearrange("o (k p) n -> p (o k) n", p=P)[:, :, c0:c0 + n])
    w_in, w_out, w1, w2 = at("w_in"), at("w_out"), at("w_ff1"), at("w_ff2")
    nat_w = [(NAT0 - 8, 476), (NAT0 - 8 + 476, 476), (NAT0 - 8 + 952, NAT + 8 - 952)]
    plan = [chunk(w_in, 0, 512), chunk(w_in, 512, 512), chunk(w_in, 1024, 512), chunk(w_in, 1536, 512)]
    plan += [chunk(w_in, a, n) for a, n in nat_w]
    plan += [(lambda slot: slot[:, :].rearrange("p (c j h) -> p c j h", c=2, j=16),
              *(at("cmp_w1").rearrange("o c (j q) h -> c q (o j) h", q=P)[c] for c in range(2)))]
    plan += [chunk(w_out, 512 * c, 512) for c in range(2)]
    plan += [chunk(w1, 512 * c, 512) for c in range(8)]
    plan += [(lambda slot: slot[:, :].rearrange("p (f n) -> p f n", f=4),
              w2.rearrange("o (c f p) n -> c p (o f) n", p=P, f=4)[c]) for c in range(8)]

    hn = sb["hn"]
    hT = sb["hT"]
    QKp, qk = sb["QKp"], sb["qk"]
    arena = sb["arena"]
    QN = arena[:, 0:3072].rearrange("p (t s d) -> p t s d", t=NT, d=HD)
    QT = arena[:, 3072:6144].rearrange("p (s n) -> p s n", n=S)
    sig = arena[:, 6144:8192]
    uT = arena[:, :].rearrange("p (f n) -> p f n", n=S)
    v_aug, og, N = sb["v_aug"], sb["og"], sb["N"]
    sq = sb["sq"]
    attn = sb["attn"]
    small = sb["small"]
    at_small = [0]

    def sm(n, rows=P):
        a = at_small[0]
        at_small[0] += n
        return small[0:rows, a:a + n]

    par = st.count()
    rows = sb["rows"]
    for r, name, n in ((0, "conv_qk", 4), (4, "norm_mix", 1), (5, "norm_ffn", 1)):
        act.dma(par, rows[r:r + n, :], at(name).rearrange("o (a n) -> (o a) n", a=1) if n == 1 else at(name).rearrange("o a n -> (o a) n"))
    act.dma(par, rows[6:7, 0:MW], at("m_norm"))
    pe_rows = sb["pe_rows"]
    act.dma(par, pe_rows[0:32, :], at("cmp_pe").rearrange("o k (j two) d -> (o k j) (two d)", two=2))
    g6 = sb["g6"]
    act.dma(par, g6[:, 0:2, :], at("moba_qk_norm").rearrange("o a d -> o (a d)").to_broadcast([P, 2 * HD]).rearrange("p (a d) -> p a d", a=2))
    act.dma(par, g6[:, 2, :], at("nsa_q_norm").to_broadcast([P, HD]))
    act.dma(par, g6[:, 3:6, :], at("nsa_k_norm").rearrange("o a d -> o (a d)").to_broadcast([P, 3 * HD]).rearrange("p (a d) -> p a d", a=3))
    cw2 = sb["cw2"]
    act.dma(par, cw2[:, :, :], at("cmp_w2").rearrange("o k h d -> h (o k) d"))
    bif = sm(2, 4)
    have_par = act.dma(par, bif, at("b_if").rearrange("o (g h) -> h (o g)", g=2), scattered=True)
    ws = Stream(st, ring, plan)

    cols = sb["cols"]
    i, ps, free = st.ps.take()
    pc = ps[:, 0, 0:64].rearrange("p (k r) -> p k r", r=8)
    t = pe.do(turned([(pc[:, k, 0:7 if k < 4 else 6], rows[0:7 if k < 4 else 6, k * P:(k + 1) * P]) for k in range(KT)]
                     + [(ps[:, 0, 64:96], pe_rows[0:32, :])], ident), have_par, free)
    have_cols = dve.do(cp(cols[:, 0:4, 0:7], pc[:, 0:4, 0:7]), t)
    have_cols = dve.do(cp(cols[:, 4:8, 0:6], pc[:, 4:8, 0:6]), t)
    peT = sm(32)
    have_pe = dve.do(cp(peT, ps[:, 0, 64:96]), t)
    st.ps.done(i, have_pe)

    def norm_to_T(gain_col, *after):
        ss, rs = sm(NT), sm(NT)
        a = [act.do(af(hn[:, t, :], x[:, t, :], ACT.Square, acc=ss[:, t:t + 1]), *after) for t in range(NT)]
        r = rms_scale(st, rs, ss, D, NT, C("m05")[:, 0:NT], a)
        ready = []
        for t in range(NT):
            b = dve.do(ts(hn[:, t, :], x[:, t, :], rs[:, t:t + 1], None, ALU.mult), r)
            i, ps, free = st.ps.take()
            c = pe.do(turned([(ps[:, k // 4, (k % 4) * P:(k % 4 + 1) * P], hn[:, t, k * P:(k + 1) * P]) for k in range(KT)], ident), b, free)
            d = dve.do(tt(hT[:, :, t * P:(t + 1) * P], flat(ps, "p b (k n) -> p (b k) n", k=4),
                          wide(cols[:, :, gain_col:gain_col + 1], [P, KT, P]), ALU.mult), c, have_cols)
            st.ps.done(i, d)
            ready.append(d)
        return ready

    ready_h = norm_to_T(4)

    pad0 = dve.do(lambda e: e.memset(QKp[:, :, 0:3], 0.0))
    for c in range(2):
        w, landed = ws.take()
        last = []
        for half in range(2):
            i, ps, free = st.ps.take()
            t = pe.do(mm_group([(ps[:, 0, b * S:(b + 1) * S],
                                 [(w[:, k, (2 * half + b) * P:(2 * half + b + 1) * P], hT[:, k, :]) for k in range(KT)])
                                for b in range(2)]), landed, ready_h, free)
            blk = 4 * c + 2 * half
            e = act.do(af(QKp[:, blk:blk + 2, 3:3 + S], ps[:, 0, :].rearrange("p (b n) -> p b n", b=2), ACT.Copy), t)
            st.ps.done(i, e)
            last.append(e)
            for b in range(blk, blk + 2):
                y = dve.do(ts(qk[:, b, :], QKp[:, b, 0:S], cols[:, b, 0:1], None, ALU.mult), e, pad0, have_cols)
                for j in range(1, 4):
                    y = dve.do(stt(qk[:, b, :], QKp[:, b, j:j + S], cols[:, b, j:j + 1], qk[:, b, :], ALU.mult, ALU.add), y)
        ws.done(t)
    qkf = qk[:, :, :].rearrange("p b n -> p (b n)")
    t = sigmoid_of(st, sig, qkf, y)
    have_qk = dve.do(tt(qkf, qkf, sig, ALU.mult), t)

    def natural(out, w, landed, c0, n, off=0):
        i, ps, free = st.ps.take()
        t = pe.do(mm_group([(ps[:, t, 0:n], [(hT[:, k, t * P:(t + 1) * P], w[:, k, c0:c0 + n]) for k in range(KT)])
                            for t in range(NT)]), landed, ready_h, free)
        return i, ps, t

    w, landed = ws.take()
    i, ps, t = natural(None, w, landed, 0, MW)
    ones = dve.do(lambda e: e.memset(v_aug[:, :, :, MD:MD + 1], 1.0))
    have_v = act.do(af(v_aug[:, :, :, 0:MD], ps[:, :, :].rearrange("p t (h d) -> p t h d", h=MH), ACT.Copy), t)
    st.ps.done(i, have_v)
    ws.done(t)
    w, landed = ws.take()
    i, ps, t = natural(None, w, landed, 0, MW)
    t2 = dve.do(ts(og[:, :, :], ps[:, :, :], -EXP_MAX, None, ALU.max), t)
    st.ps.done(i, t2)
    ws.done(t)
    t2 = act.do(af(og[:, :, :], og[:, :, :], ACT.Exp, scale=-1.0), t2)
    t2 = dve.do(ts(og[:, :, :], og[:, :, :], 1.0, None, ALU.add), t2)
    have_og = dve.do(lambda e: e.reciprocal(og[:, :, :], og[:, :, :]), t2)

    w, landed = ws.take()
    gi, gps, free = st.ps.take()
    gates = pe.do(mm_group([(gps[0:MH, 0, g * S:(g + 1) * S], [(w[:, k, g * MH:(g + 1) * MH], hT[:, k, :]) for k in range(KT)])
                            for g in range(2)]), landed, ready_h, free)
    i, ps, t = natural(None, w, landed, 8, 468)
    e = act.do(af(N[:, :, 0:468], ps[:, :, 0:468], ACT.Copy), t)
    st.ps.done(i, e)
    ws.done(t)
    base = 468
    for c in range(2):
        w, landed = ws.take()
        n = nat_w[c + 1][1]
        i, ps, t = natural(None, w, landed, 0, n)
        have_N = act.do(af(N[:, :, base:base + n], ps[:, :, 0:n], ACT.Copy), t)
        st.ps.done(i, have_N)
        ws.done(t)
        base += n
    hT_free = t

    rI, rF, rA, rL, rB, rC, rM, rN = (sb["sq"][0:MH, j * S:(j + 1) * S] for j in range(8))
    t = dve.do(ts(rI, gps[0:MH, 0, 0:S], bif[:, 0:1], None, ALU.add), gates)
    f = dve.do(ts(rF, gps[0:MH, 0, S:2 * S], bif[:, 1:2], None, ALU.add), gates)
    st.ps.done(gi, t, f)
    t = dve.do(stt(rA, rF, -1.0, rF, ALU.mult, ALU.max), f)
    t = act.do(af(rA, rA, ACT.Exp, scale=-1.0), t)
    t = act.do(af(rL, rA, ACT.Ln, bias=1.0), t)
    t = dve.do(stt(rL, rF, 0.0, rL, ALU.min, ALU.subtract), t)
    t = dve.do(lambda e: e.tensor_tensor_scan(rB, C("ones")[0:MH, :], rL, 0.0, ALU.mult, ALU.add), t)
    t = dve.do(tt(rC, rI, rB, ALU.subtract), t)
    m = dve.do(lambda e: e.tensor_tensor_scan(rM, rC, rC, 0.0, ALU.max, ALU.max), t)
    n = dve.do(stt(rN, rB, -1.0, rM, ALU.mult, ALU.subtract), m)
    i, ps, free = st.ps.take()
    cn = ps[:, 0, 0:16].rearrange("p (a t h) -> p a t h", a=2, t=NT)
    t = pe.do(turned([(cn[:, a, t, :], (rC, rN)[a][:, t * P:(t + 1) * P]) for a in range(2) for t in range(NT)], ident), n, free)
    cc = sm(16).rearrange("p (a t h) -> p a t h", a=2, t=NT)
    have_cc = dve.do(cp(cc, cn), t)
    st.ps.done(i, have_cc)
    em = sm(8).rearrange("p (t h) -> p t h", t=NT)
    have_em = act.do(af(em, cc[:, 1], ACT.Exp), have_cc)
    W0, W1 = sb["W0"], sb["W1"]
    bi, bps, free = st.ps.take()
    sel = C("sel").rearrange("p (h m) -> p h m", h=4)
    t = pe.do(mm_group([(bps[:, h // 2, (h % 2) * S:(h % 2 + 1) * S], [(sel[0:MH, h, :], rM)]) for h in range(MH)]), m, free)
    Mb = flat(bps, "p b (h n) -> p (b h) n", h=2)
    causT = wide(C("causT"), [P, MH, P], 1)
    a0 = dve.do(tt(W0[:, :, 0:P], causT, Mb[:, :, 0:P], ALU.subtract), t)
    a1 = dve.do(tt(W1[:, :, :], causT, Mb[:, :, P:S], ALU.subtract), t)
    for h in range(MH):
        w00 = act.do(af(W0[:, h, 0:P], W0[:, h, 0:P], ACT.Exp, bias=cc[:, 0, 0, h:h + 1]), a0, have_cc)
        w01 = act.do(af(W0[:, h, P:S], Mb[:, h, P:S], ACT.Exp, bias=cc[:, 0, 0, h:h + 1], scale=-1.0), a0, a1, have_cc)
        w11 = act.do(af(W1[:, h, :], W1[:, h, :], ACT.Exp, bias=cc[:, 0, 1, h:h + 1]), a1, have_cc)
    st.ps.done(bi, a0, a1, w01)
    i0, p0, free0 = st.ps.take()
    i1, p1, free1 = st.ps.take()
    s0 = flat(p0, "p b (h n) -> p (b h) n", h=2)
    s1 = p1[:, 0, :].rearrange("p (h n) -> p h n", h=MH)
    t0 = pe.do(mm_group([(s0[:, h, :], [(qk[:, MH + h, 0:P], qk[:, h, :])]) for h in range(MH)]), have_qk, free0)
    t1 = pe.do(mm_group([(s1[:, h, :], [(qk[:, MH + h, P:S], qk[:, h, P:S])]) for h in range(MH)]), have_qk, free1)
    u0 = dve.do(stt(W0[:, :, :], s0, MD ** -0.5, W0[:, :, :], ALU.mult, ALU.mult), t0, w01)
    u1 = dve.do(stt(W1[:, :, :], s1, MD ** -0.5, W1[:, :, :], ALU.mult, ALU.mult), t1, w11)
    st.ps.done(i0, u0)
    st.ps.done(i1, u1)
    dn = sm(8).rearrange("p (t h) -> p t h", t=NT)
    mix = hn
    for t in range(NT):
        i, ps, free = st.ps.take()
        o = lambda h: ps[:, h // 2, (h % 2) * (MD + 1):(h % 2 + 1) * (MD + 1)]
        if t == 0:
            terms = [(o(h), [(W0[:, h, 0:P], v_aug[:, 0, h, :])]) for h in range(MH)]
        else:
            terms = [(o(h), [(W0[:, h, P:S], v_aug[:, 0, h, :]), (W1[:, h, :], v_aug[:, 1, h, :])]) for h in range(MH)]
        a = pe.do(mm_group(terms), u0, u1, have_v, ones, free)
        view = ps[:, :, 0:2 * (MD + 1)].rearrange("p b (j c) -> p b j c", j=2)
        d4 = dn[:, t, :].rearrange("p (b j) -> p b j", b=2)
        b = dve.do(stt(d4, view[:, :, :, MD], -1.0, em[:, t, :].rearrange("p (b j) -> p b j", b=2), ALU.mult, ALU.max), a, have_em)
        b = dve.do(tt(d4, view[:, :, :, MD], d4, ALU.max), b)
        b = dve.do(lambda e, d4=d4: e.reciprocal(d4, d4), b)
        hm = dve.do(tt(mix[:, t, 0:MW].rearrange("p (b j d) -> p b j d", b=2, j=2), view[:, :, :, 0:MD],
                       wide(d4, [P, 2, 2, MD], 3), ALU.mult), b, hT_free)
        st.ps.done(i, hm)
    m4 = mix[:, :, 0:MW].rearrange("p t (h d) -> p t h d", h=MH)
    scr = sq[:, 0:NT * MW].rearrange("p (t n) -> p t n", t=NT)
    t = dve.do(tt(scr, mix[:, :, 0:MW], mix[:, :, 0:MW], ALU.mult), hm)
    ssm = sm(8)
    t = dve.do(red(ssm, sq[:, 0:NT * MW].rearrange("p (g d) -> p g d", d=MD), ALU.add), t)
    sq_free = t
    t = rms_scale(st, ssm, ssm, MD, 8, C("m05")[:, 0:8], t)
    t = dve.do(tt(m4, m4, wide(ssm.rearrange("p (t h) -> p t h", t=NT), [P, NT, MH, MD], 3), ALU.mult), t)
    mixed = [dve.do(tt(mix[:, :, 0:MW], mix[:, :, 0:MW], og[:, :, :], ALU.mult), t, have_og)]

    heads = N[:, :, 0:NG * HD].rearrange("p t (g d) -> p t g d", d=HD)
    sq4 = sq[:, :].rearrange("p (t n) -> p t n", t=NT)
    t = dve.do(tt(sq4, N[:, :, 0:NG * HD], N[:, :, 0:NG * HD], ALU.mult), have_N, sq_free)
    rs = sm(NT * NG)
    t = dve.do(red(rs, sq[:, :].rearrange("p (g d) -> p g d", d=HD), ALU.add), t)
    t = rms_scale(st, rs, rs, HD, NT * NG, C("m05")[:, 0:NT * NG], t)
    rs3 = rs.rearrange("p (t g) -> p t g", t=NT)
    t1 = dve.do(ts(rs3[:, :, 0:4], rs3[:, :, 0:4], HD ** -0.5, None, ALU.mult), t)
    t2 = dve.do(ts(rs3[:, :, 12:16], rs3[:, :, 12:16], HD ** -0.5, None, ALU.mult), t)
    sqh = sq[:, :].rearrange("p (t g d) -> p t g d", t=NT, d=HD)
    for tl in range(NT):
        t = dve.do(tt(sqh[:, tl], heads[:, tl], wide(rs3[:, tl], [P, NG, HD], 2), ALU.mult), t1, t2)
    for s0_, n_, g0_, gain in ((0, 4, 0, 0), (4, 4, 4, 1), (8, 4, 12, 2), (16, 4, 12, 2), (12, 2, 18, 4), (14, 2, 20, 5)):
        for tl in range(NT):
            src = sqh[:, tl, g0_:g0_ + n_, :] if n_ == 4 else sqh[:, tl, g0_:g0_ + 1, :].to_broadcast([P, 2, HD])
            slots = dve.do(tt(QN[:, tl, s0_:s0_ + n_, :], src, g6[:, gain:gain + 1, :].to_broadcast([P, n_, HD]), ALU.mult), t, have_par)
    for c in range(2):
        for tl in range(NT):
            slots = dve.do(cp(QN[:, tl, 20 + 2 * c:22 + 2 * c, :], heads[:, tl, 16 + c:17 + c, :].to_broadcast([P, 2, HD])), have_N)
    rope = attn[:, 0:1024].rearrange("p (a s d) -> p a s d", a=4, d=8)
    for tl in range(NT):
        cos = wide(C("cos1")[:, tl * 8:(tl + 1) * 8], [P, 16, 8], 1)
        sin = wide(C("sin1")[:, tl * 8:(tl + 1) * 8], [P, 16, 8], 1)
        x1, x2 = QN[:, tl, 0:16, 0:8], QN[:, tl, 0:16, 8:16]
        ra, rb, rc, rd = (attn[:, 512 * tl + 128 * j:512 * tl + 128 * (j + 1)].rearrange("p (s d) -> p s d", d=8) for j in range(4))
        dve.do(tt(ra, x1, cos, ALU.mult), slots)
        dve.do(tt(rb, x2, sin, ALU.mult), slots)
        dve.do(tt(rc, x2, cos, ALU.mult), slots)
        u = dve.do(tt(rd, x1, sin, ALU.mult), slots)
        dve.do(tt(x1, ra, rb, ALU.subtract), u)
        roped = dve.do(tt(x2, rc, rd, ALU.add), u)
    have_QT = []
    for q in range(6):
        i, ps, free = st.ps.take()
        a = pe.do(turned([(ps[:, b, t * P:(t + 1) * P], QN[:, t, 4 * q + 2 * b:4 * q + 2 * b + 2, :].rearrange("p s d -> p (s d)"))
                          for b in range(2) for t in range(NT)], ident), roped, free)
        b = act.do(af(QT[:, 2 * q:2 * q + 2, :], ps[:, :, 0:S], ACT.Copy), a)
        st.ps.done(i, b)
        have_QT.append(b)

    cb = sb["cb"]
    cb5 = cb[:, :].rearrange("p (c j n) -> p c j n", c=2, j=16)
    for c in range(2):
        for half in range(2):
            r = slice(64 * half, 64 * half + 64)
            tok = QT[r, 10 + c, :].rearrange("p (n q) -> p q n", q=16)
            for g in range(2):
                cbs = dve.do(tt(cb5[r, c, 8 * g:8 * g + 8, :], tok[:, half::2, g:g + NC_CMP],
                                wide(peT[r, 16 * c + 8 * g:16 * c + 8 * g + 8], [64, 8, NC_CMP], 2), ALU.add), have_QT, have_pe)
    w, landed = ws.take()
    i, ps, free = st.ps.take()
    t = pe.do(mm_group([(ps[:, 0, 16 * c:16 * c + NC_CMP], [(w[:, c, j, :], cb5[:, c, j, :]) for j in range(16)]) for c in range(2)]), cbs, landed, free)
    ws.done(t)
    hid = sm(32).rearrange("p (c n) -> p c n", c=2)[:, :, 0:NC_CMP]
    sg = sm(32).rearrange("p (c n) -> p c n", c=2)[:, :, 0:NC_CMP]
    t = act.do(af(hid, ps[:, 0, 0:32].rearrange("p (c n) -> p c n", c=2)[:, :, 0:NC_CMP], ACT.Copy), t)
    st.ps.done(i, t)
    t = sigmoid_of(st, sg, hid, t)
    t = dve.do(tt(hid, hid, sg, ALU.mult), t)
    i, ps, free = st.ps.take()
    t = pe.do(mm_group([(ps[0:NC_CMP, 0, c * HD:(c + 1) * HD], [(hid[:, c, :], cw2[:, c, :])]) for c in range(2)]), t, have_par, free)
    kv = sb["kv"]
    kcn, vcn, ksq = kv[0:NC_CMP, 0:HD], kv[0:NC_CMP, HD:2 * HD], kv[0:NC_CMP, 2 * HD:4 * HD]
    t = dve.do(cp(kv[0:NC_CMP, 0:2 * HD], ps[0:NC_CMP, 0, 0:2 * HD]), t)
    have_vc = t
    st.ps.done(i, t)
    kss = sm(1)[0:NC_CMP]
    t = dve.do(tt(ksq[:, 0:HD], kcn, kcn, ALU.mult), t)
    t = dve.do(red(kss, ksq[:, 0:HD], ALU.add), t)
    t = rms_scale(st, kss, kss, HD, 1, C("m05")[0:NC_CMP, 0:1], t)
    t = dve.do(stt(ksq[:, 0:HD], kcn, kss, g6[0:NC_CMP, 3, :], ALU.mult, ALU.mult), t)
    t = dve.do(cp(ksq[:, HD:2 * HD], ksq[:, 0:HD]), t)
    i, ps, free = st.ps.take()
    t = pe.do(turned([(ps[:, 0, 0:NC_CMP], ksq)], ident), t, free)
    kcT = sm(16)
    t = dve.do(cp(kcT[:, 0:NC_CMP], ps[:, 0, 0:NC_CMP]), t)
    st.ps.done(i, t)
    half_of = lambda h: slice(64 * (h % 2), 64 * (h % 2) + 64)
    i, ps, free = st.ps.take()
    sc = ps[:, :, 0:64].rearrange("p b (t j n) -> p b t j n", t=NT, j=2)
    t = pe.do(mm_group([(sc[:, h % 2, t, h // 2, 0:NC_CMP], [(QT[half_of(h), 8 + h // 2, t * P:(t + 1) * P], kcT[half_of(h), 0:NC_CMP])])
                        for t in range(NT) for h in range(4)]), t, have_QT, free)
    pcb = sm(8 * NC_CMP)
    pc5 = pcb.rearrange("p (b t j n) -> p b t j n", b=2, t=NT, j=2)
    pc3 = pcb.rearrange("p (g n) -> p g n", g=8)
    per_t = lambda name: wide(C(name).rearrange("p (t n) -> p t n", t=NT), [P, NT, 2, NC_CMP], 2)
    s1 = dve.do(tt(pc5[:, 0], sc[:, 0, :, :, 0:NC_CMP], per_t("cmp_add"), ALU.add), t)
    t = dve.do(tt(pc5[:, 1], sc[:, 1, :, :, 0:NC_CMP], per_t("cmp_add"), ALU.add), t)
    st.ps.done(i, t)
    cm, cs = sm(8), sm(8)
    t = dve.do(red(cm, pc3, ALU.max), t)
    t = dve.do(tt(pc3, pc3, wide(cm, [P, 8, NC_CMP], 2), ALU.subtract), t)
    t = act.do(af(pcb, pcb, ACT.Exp), t)
    t = dve.do(red(cs, pc3, ALU.add), t)
    t = dve.do(lambda e: e.reciprocal(cs, cs), t)
    t = dve.do(tt(pc3, pc3, wide(cs, [P, 8, NC_CMP], 2), ALU.mult), t)
    t1 = dve.do(tt(pc5[:, 0], pc5[:, 0], per_t("cmp_on"), ALU.mult), t)
    t = dve.do(tt(pc5[:, 1], pc5[:, 1], per_t("cmp_on"), ALU.mult), t)
    i, ps, free = st.ps.take()
    t = pe.do(turned([(ps[0:NC_CMP, g // 4, (g % 4) * P:(g % 4 + 1) * P], pc3[:, g, :]) for g in range(8)], ident), t, free)
    pcT = sq[0:NC_CMP, 0:1024]
    t = act.do(af(pcT.rearrange("p (b n) -> p b n", b=2), ps[0:NC_CMP, :, :], ACT.Copy), t, slots)
    st.ps.done(i, t)
    i, ps, free = st.ps.take()
    t = pe.do(mm_group([(ps[:, 0, (4 * tl + 2 * j + b) * HD:(4 * tl + 2 * j + b + 1) * HD],
                         [(pcT[:, (4 * b + 2 * tl + j) * P:(4 * b + 2 * tl + j + 1) * P], vcn)]) for b in range(2) for tl in range(NT) for j in range(2)]), t, have_vc, free)
    gt = sm(24).rearrange("p (t g) -> p t g", t=NT)
    g1 = sigmoid_of(st, gt, N[:, :, NG * HD:NG * HD + 12], have_N)
    gate = lambda t, b: wide(gt[:, t, 4 * b:4 * b + 4], [P, 4, HD], 2)
    yn = lambda t: mix[:, t, 768:1024].rearrange("p (h d) -> p h d", h=4)
    for tl in range(NT):
        have_oc = dve.do(tt(yn(tl), ps[:, 0, tl * S:(tl + 1) * S].rearrange("p (h d) -> p h d", h=4), gate(tl, 0), ALU.mult), t, g1, hT_free)
    st.ps.done(i, have_oc)

    bufs = Turns([attn[:, 0:3072], attn[:, 3072:6144]])
    bufs.free = [[roped], []]
    tmp = sq[:, 1024:1024 + S].rearrange("p (h d) -> p h d", h=4)
    stat = sm(2 * 8)
    for f, (q0, k0, v_of) in enumerate(((0, lambda h: 2 + h // 2, lambda h: 8 + h), (4, lambda h: 6, lambda h: 19), (4, lambda h: 7, lambda h: 21))):
        for t in range(NT):
            nk = P * (t + 1)
            bi, buf, bfree = bufs.take()
            sc, pT = buf[:, 0:4 * nk].rearrange("p (h n) -> p h n", h=4), buf[:, 1024:1024 + 4 * nk]
            pr = buf[:, 2048:2048 + 4 * nk].rearrange("p (h n) -> p h n", h=4)
            mx, den = stat[:, 8 * bi:8 * bi + 4], stat[:, 8 * bi + 4:8 * bi + 8]
            i, ps, free = st.ps.take()
            s_of = flat(ps, "p b (h n) -> p (b h) n", h=2)[:, :, 0:nk]
            a = pe.do(mm_group([(s_of[:, 2 * (h % 2) + h // 2, :], [(QT[half_of(h), q0 + h // 2, t * P:(t + 1) * P], QT[half_of(h), k0(h), 0:nk])])
                                for h in range(4)]), have_QT, free)
            a = dve.do(tt(sc, s_of, wide(C("caus")[:, S - nk:S], [P, 4, nk], 1), ALU.add), a, bfree)
            st.ps.done(i, a)
            a = dve.do(red(mx, sc, ALU.max, negate=True), a)
            for g in range(4):
                h = 2 * (g % 2) + g // 2
                b = act.do(af(pr[:, g, :], sc[:, g, :], ACT.Exp, bias=mx[:, g:g + 1], acc=den[:, h:h + 1]), a, bfree)
            r = dve.do(lambda e, den=den: e.reciprocal(den, den), b)
            i, ps, free = st.ps.take()
            nb = 4 * (t + 1)
            c = pe.do(turned([(ps[:, j // 4, (j % 4) * P:(j % 4 + 1) * P], pr[:, j // (t + 1), (j % (t + 1)) * P:(j % (t + 1) + 1) * P])
                              for j in range(nb)], ident), b, free)
            c2 = act.do(af(pT.rearrange("p (b n) -> p b n", n=512), ps[:, 0:t + 1, :], ACT.Copy), c, bfree)
            st.ps.done(i, c2)
            i, ps, free = st.ps.take()
            d = pe.do(mm_group([(ps[:, 0, h * HD:(h + 1) * HD],
                                 [(pT[:, ((2 * (h % 2) + h // 2) * (t + 1) + kt) * P:((2 * (h % 2) + h // 2) * (t + 1) + kt + 1) * P], heads[:, kt, v_of(h), :]) for kt in range(t + 1)])
                                for h in range(4)]), c2, free)
            o = ps[:, 0, 0:S].rearrange("p (h d) -> p h d", h=4)
            if f == 0:
                e = dve.do(tt(mix[:, t, 512:768].rearrange("p (h d) -> p h d", h=4), o, wide(den, [P, 4, HD], 2), ALU.mult), d, r, hT_free)
            else:
                e = dve.do(tt(tmp, o, wide(den, [P, 4, HD], 2), ALU.mult), d, r)
                g = dve.do(tt(tmp, tmp, gate(t, f), ALU.mult), e)
                g = dve.do(tt(yn(t), yn(t), tmp, ALU.add), g, have_oc)
                mixed.append(g)
            st.ps.done(i, e)
            bufs.done(bi, e)
            mixed.append(e)

    ready = []
    for t in range(NT):
        i, ps, free = st.ps.take()
        c = pe.do(turned([(ps[:, k // 4, (k % 4) * P:(k % 4 + 1) * P], mix[:, t, k * P:(k + 1) * P]) for k in range(KT)], ident), mixed, free)
        d = dve.do(tt(hT[:, 0:4, t * P:(t + 1) * P], ps[:, 0, :].rearrange("p (k n) -> p k n", k=4),
                      wide(cols[:, 0:4, 6:7], [P, 4, P]), ALU.mult), c)
        d2 = act.do(af(hT[:, 4:8, t * P:(t + 1) * P], ps[:, 1, :].rearrange("p (k n) -> p k n", k=4), ACT.Copy), c)
        st.ps.done(i, d, d2)
        ready += [d, d2]
    ready_h = ready
    for c in range(2):
        w, landed = ws.take()
        i, ps, t = natural(None, w, landed, 0, 512)
        ws.done(t)
        xv = x[:, :, c * 512:(c + 1) * 512]
        added = dve.do(tt(xv, xv, ps[:, :, :], ALU.add), t, ready)
        st.ps.done(i, added)

    ready_h = norm_to_T(5, added)
    rl = Turns([attn[:, 0:1024], attn[:, 1024:2048]])
    squared = []
    for c in range(8):
        w, landed = ws.take()
        i, ps, free = st.ps.take()
        t = pe.do(mm_group([(ps[:, b // 2, (b % 2) * S:(b % 2 + 1) * S],
                             [(w[:, k, b * P:(b + 1) * P], hT[:, k, :]) for k in range(KT)]) for b in range(4)]), landed, ready_h, free)
        ws.done(t)
        ri, rbuf, rfree = rl.take()
        a = act.do(af(rbuf.rearrange("p (b n) -> p b n", b=2), ps[:, :, :], ACT.Relu), t, rfree)
        st.ps.done(i, a)
        b = dve.do(tt(uT[:, 4 * c:4 * c + 4, :].rearrange("p f n -> p (f n)"), rbuf, rbuf, ALU.mult), a)
        rl.done(ri, b)
        squared.append(b)
    (i0, p0, f0), (i1, p1, f1) = st.ps.take(), st.ps.take()
    acc = (p0, p1)
    for c in range(8):
        w, landed = ws.take()

        def fn(e, c=c, w=w):
            for f in range(4):
                for t in range(NT):
                    for half in range(2):
                        last = e.matmul(acc[t][:, half, :], uT[:, 4 * c + f, t * P:(t + 1) * P], w[:, f, half * 512:(half + 1) * 512],
                                        start=(c == 0 and f == 0), stop=(c == 7 and f == 3))
            return last
        t = pe.do(fn, squared[c], landed, f0, f1)
        ws.done(t)
    for tl in range(NT):
        xv = x[:, tl, :].rearrange("p (b n) -> p b n", b=2)
        fin = dve.do(tt(xv, xv, acc[tl][:, :, :], ALU.add), t)
    return fin



def in_turn(steps, width):
    waiting, running = list(steps), []
    while waiting or running:
        while waiting and len(running) < width:
            running.append(waiting.pop(0))
        for g in list(running):
            try:
                next(g)
            except StopIteration:
                running.remove(g)


def attention_block(st, sb, A, C, xs, layer):
    pe, dve, act, pool, sp = st.pe, st.dve, st.act, st.pool, st.sp
    last = layer == DEPTH - 1
    ident, sel = C("ident"), C("sel").rearrange("p (h m) -> p h m", h=4)
    chunk = lambda w, c: (lambda slot: slot[:, :].rearrange("p (k n) -> p k n", k=KT),
                          w.rearrange("(k p) n -> p k n", p=P)[:, :, c * 512:(c + 1) * 512])
    ada, wqkv, wo, wq = A["ada_w_2"][layer], A["w_qkv_2"][layer], A["w_o_2"][layer], A["peer_w_q_2"][layer]
    plan = [chunk(ada, c) for c in range(6)] + [chunk(wqkv, c) for c in range(3)] + [chunk(wo, c) for c in range(2)]
    plan += [chunk(ada, c) for c in range(6, 12)] + [chunk(wq, c) for c in range(4)]
    q_tiles = [0, 1] if last else [0, 1, 2, 3]
    mod, H, hT, Y, QT, bufs, small = sb["mod"], sb["H"], sb["hT2"], sb["Y"], sb["QT2"], sb["bufs"], sb["small2"]
    used = [0]

    def sm(n):
        used[0] += n
        return small[:, used[0] - n:used[0]]

    par = st.count()
    crow, gains, qkg, sub, sink = sb["crow"], sb["gains"], sb["qkg"], sb["sub"], sb["sink"]
    act.dma(par, crow[:, 0, :], A["c_2"].rearrange("o (k p) -> (o k) p", p=P))
    act.dma(par, crow[:, 1, :], A["c_ctx_2"].rearrange("(k p) -> k p", p=P))
    for j, name in enumerate(("norm1_gain_2", "norm2_gain_2")):
        act.dma(par, gains[:, j, :], A[name][layer:layer + 1, :].to_broadcast([P, D]))
    for j, name in enumerate(("q_norm_gain_2", "k_norm_gain_2")):
        act.dma(par, qkg[:, j, :], A[name][layer:layer + 1, :].to_broadcast([P, HD2]))
    act.dma(par, sink[:, :], A["attn_sinks_2"][0:1, :].to_broadcast([P, H2]))
    have = act.dma(par, sub[:, 0:2, :], A["peer_sub_keys_2"][layer].rearrange("a k d -> k a d"))
    bias = Turns([(b, st.count()) for b in (sb["brow"][:, j, :] for j in range(3))])
    ws = Stream(st, sb["ring"], plan)

    i, ps, free = st.ps.take()
    t = pe.do(turned([(ps[:, 0, 8 * v:8 * v + 8], crow[:, v, :]) for v in range(2)]
                     + [(ps[:, 0, P * (a + 1):P * (a + 2)], sub[:, a, :]) for a in range(2)], ident), have, free)
    cT = sm(16)
    e = dve.do(cp(cT, ps[:, 0, 0:16]), t)
    have_sub = dve.do(cp(sub[:, 2:4, :].rearrange("p a n -> p (a n)"), ps[:, 0, P:3 * P]), t)
    st.ps.done(i, have_sub)
    sg = sm(16)
    t = sigmoid_of(st, sg, cT, e)
    have_c = dve.do(tt(cT, cT, sg, ALU.mult), t)
    c_of = cT.rearrange("p (v k) -> p v k", v=2)

    mrows = Turns([sb["mrow"][:, j, :] for j in range(2)])

    def modulation(first, norm_gain, *after):
        for c in range(6):
            w, landed = ws.take()
            bi, (brow, count), bfree = bias.take()
            b = act.dma(count, brow, A["ada_b_2"][layer:layer + 1, (first + c) * 512:(first + c + 1) * 512].to_broadcast([2, 512]), bfree, *after)
            i, ps, free = st.ps.take()
            t = pe.do(mm_group([(ps[0:2, 0, :], [(c_of[:, :, k], w[:, k, :]) for k in range(KT)])]), landed, have_c, free)
            ws.done(t)
            mi, mrow, mfree = mrows.take()
            e = dve.do(tt(mrow, ps[0:2, 0, :], brow, ALU.add), t, b, mfree, *after)
            st.ps.done(i, e)
            bias.done(bi, e)
            i, ps, free = st.ps.take()
            t = pe.do(mm_group([(ps[:, v, :], [(sel[0:2, v, :], mrow)]) for v in range(2)]), e, free)
            mrows.done(mi, t)
            dst = mod[:, :, c // 2, (c % 2) * 512:(c % 2 + 1) * 512]
            if c // 2 == 1:
                for v in range(2):
                    e = dve.do(stt(dst[:, v, :], ps[:, v, :], 1.0, gains[:, norm_gain, (c % 2) * 512:(c % 2 + 1) * 512], ALU.add, ALU.mult), t, have, *after)
                made.append(e)
            else:
                e = act.do(af(dst, ps[:, :, :], ACT.Copy), t, *after)
                made.append(e)
            st.ps.done(i, e)

    def norm_modulate(tiles, *after):
        ss, rs = sm(4), sm(4)
        a = [act.do(af(H[:, g, :], xs[g], ACT.Square, acc=ss[:, g:g + 1]), *after) for g in tiles]
        n = len(tiles)
        r = rms_scale(st, rs[:, 0:n], ss[:, 0:n], D, n, C("m05")[:, 0:n], a)
        ready = []
        for g in tiles:
            t = dve.do(stt(H[:, g, :], xs[g], rs[:, g:g + 1], mod[:, g // 2, 1, :], ALU.mult, ALU.mult), r, made)
            t = dve.do(tt(H[:, g, :], H[:, g, :], mod[:, g // 2, 0, :], ALU.add), t)
            ready.append(transpose_H(g, t))
        return ready

    def transpose_H(g, *after):
        i, ps, free = st.ps.take()
        t = pe.do(turned([(ps[:, k // 4, (k % 4) * P:(k % 4 + 1) * P], H[:, g, k * P:(k + 1) * P]) for k in range(KT)], ident), *after, free)
        t = act.do(af(hT[:, :, g * P:(g + 1) * P], flat(ps, "p b (k n) -> p (b k) n", k=4), ACT.Copy), t)
        st.ps.done(i, t)
        return t

    def project(w, landed, tiles, after):
        i, ps, free = st.ps.take()
        t = pe.do(mm_group([(ps[:, j, :], [(hT[:, k, g * P:(g + 1) * P], w[:, k, :]) for k in range(KT)])
                            for j, g in enumerate(tiles)]), landed, after, free)
        return i, ps, t

    made = []
    modulation(0, 0)
    ready = norm_modulate([0, 1, 2, 3])
    have_Y = []
    for c in range(3):
        w, landed = ws.take()
        for g in (0, 2):
            if g not in q_tiles and c < 2:
                continue
            i, ps, t = project(w, landed, (g, g + 1), ready)
            e = act.do(af(Y[:, g:g + 2, c * 512:(c + 1) * 512], ps[:, :, :], ACT.Copy), t)
            st.ps.done(i, e)
            have_Y.append(e)
        ws.done(t)

    rs = sm(40)
    nq = len(q_tiles)
    parts = [(0, H2, q_tiles, 0, rs[:, 0:8 * nq]), (H2, KV2, [0, 1, 2, 3], 1, rs[:, 32:40])]
    normed = []
    for h0, nh, tiles, gain, r in parts:
        for j, g in enumerate(tiles):
            y = Y[:, g, h0 * HD2:(h0 + nh) * HD2]
            scr = QT[:, :].rearrange("p h n -> p (h n)")[:, 0:nh * HD2]
            t = dve.do(tt(scr, y, y, ALU.mult), have_Y, normed)
            t = dve.do(red(r[:, j * nh:(j + 1) * nh], scr.rearrange("p (h d) -> p h d", d=HD2), ALU.add), t)
            normed = [t]
        t = rms_scale(st, r, r, HD2, len(tiles) * nh, C("m05")[:, 0:len(tiles) * nh], t)
        if h0 == 0:
            t = dve.do(ts(r, r, HD2 ** -0.5, None, ALU.mult), t)
        for j, g in enumerate(tiles):
            y = Y[:, g, h0 * HD2:(h0 + nh) * HD2].rearrange("p (h d) -> p h d", d=HD2)
            a = dve.do(tt(y, y, wide(r[:, j * nh:(j + 1) * nh], [P, nh, HD2], 2), ALU.mult), t)
            a = dve.do(tt(y, y, qkg[:, gain:gain + 1, :].to_broadcast([P, nh, HD2]), ALU.mult), a, have)
            normed.append(a)
    tmp = bufs[:, 0:2560].rearrange("p (j h a d) -> p j h a d", j=4, h=10, a=2)
    u = None
    for g in (0, 1):
        y = Y[:, g, 0:10 * HD2].rearrange("p (h a b d) -> p h a b d", h=10, a=2, b=2)
        for a in range(2):
            y1, y2 = y[:, :, a, 0, :], y[:, :, a, 1, :]
            tab = lambda name: wide(C(name)[:, g * 64 + a * 32:g * 64 + a * 32 + 32], [P, 10, 32], 1)
            ta = [tmp[:, j, :, a, :] for j in range(4)]
            dve.do(tt(ta[0], y1, tab("cos2"), ALU.mult), normed, u)
            dve.do(tt(ta[1], y2, tab("sin2"), ALU.mult))
            dve.do(tt(ta[2], y1, tab("sin2"), ALU.mult))
            v = dve.do(tt(ta[3], y2, tab("cos2"), ALU.mult))
            dve.do(tt(y1, ta[0], ta[1], ALU.subtract), v)
            w_ = dve.do(tt(y2, ta[2], ta[3], ALU.add))
        u = w_
    have_QT = []
    for hp in range(5):
        tiles = q_tiles if hp < 4 else [0, 1, 2, 3]
        n = len(tiles) * P
        i, ps, free = st.ps.take()
        t = pe.do(turned([(ps[:, j, g * P:(g + 1) * P], Y[:, g, (2 * hp + j) * HD2:(2 * hp + j + 1) * HD2]) for j in range(2) for g in tiles], ident),
                  u, normed, free)
        t = act.do(af(QT[:, 2 * hp:2 * hp + 2, 0:n], ps[:, :, 0:n], ACT.Copy), t, normed)
        st.ps.done(i, t)
        have_QT.append(t)

    pbufs = Turns([(bufs[:, 1536 * j:1536 * j + 512], bufs[:, 1536 * j + 512:1536 * j + 1024], bufs[:, 1536 * j + 1024:1536 * j + 1536], j) for j in range(2)]
                  + [(sb["bufs3"][:, 0:512], sb["bufs3"][:, 512:1024], sb["bufs3"][:, 1024:1536], 2)])
    pbufs.free = [[u], [u], []]
    stat = sm(12)
    done = {g: [] for g in q_tiles}

    def head(g, h):
        lo = 0 if g < 2 else 2 * P
        nk = 4 * P - lo
        bi, (sc, pr, pT, j), bfree = pbufs.take()
        mx, den, ex = (stat[:, 4 * j + a:4 * j + a + 1] for a in range(3))
        i, ps, free = st.ps.take()
        a = pe.do(mm_group([(ps[:, 0, 0:nk], [(QT[:, h, g * P:(g + 1) * P], QT[:, H2 + h // 4, lo:4 * P])])]), have_QT, free)
        src = ps[:, 0, 0:nk]
        if last:
            a = dve.do(tt(sc, src, C("win")[:, g * 512:(g + 1) * 512], ALU.add), a, bfree)
            st.ps.done(i, a)
            src = sc
        a = dve.do(red(mx, src, ALU.max, negate=True), a, bfree)
        if last:
            a = dve.do(stt(mx, sink[:, h:h + 1], -1.0, mx, ALU.mult, ALU.min), a, have)
        b = act.do(af(pr[:, 0:nk], src, ACT.Exp, bias=mx, acc=den), a, bfree)
        if not last:
            st.ps.done(i, b)
        yield
        if last:
            s_ = act.do(af(ex, sink[:, h:h + 1], ACT.Exp, bias=mx), a)
            b2 = dve.do(tt(den, den, ex, ALU.add), b, s_)
        else:
            b2 = b
        r = dve.do(lambda e: e.reciprocal(den, den), b2)
        i, ps, free = st.ps.take()
        c = pe.do(turned([(ps[:, 0, k * P:(k + 1) * P], pr[:, k * P:(k + 1) * P]) for k in range(nk // P)], ident), b, free)
        c = (act if h % 2 else dve).do((af(pT[:, 0:nk], ps[:, 0, 0:nk], ACT.Copy) if h % 2 else cp(pT[:, 0:nk], ps[:, 0, 0:nk])), c, bfree)
        st.ps.done(i, c)
        yield
        i, ps, free = st.ps.take()
        d = pe.do(mm_group([(ps[:, 0, 0:HD2], [(pT[:, k * P:(k + 1) * P], Y[:, k + lo // P, (H2 + KV2 + h // 4) * HD2:(H2 + KV2 + h // 4 + 1) * HD2])
                                               for k in range(nk // P)])]), c, free)
        e = dve.do(ts(H[:, g, h * HD2:(h + 1) * HD2], ps[:, 0, 0:HD2], den, None, ALU.mult), d, r, ready)
        st.ps.done(i, e)
        pbufs.done(bi, e)
        done[g].append(e)
        yield

    in_turn([head(g, h) for g in q_tiles for h in range(H2)], 3)
    ready = [transpose_H(g, done[g]) for g in q_tiles]

    prod = Turns([bufs[:, 0:1024].rearrange("p (t n) -> p t n", t=2), bufs[:, 1024:2048].rearrange("p (t n) -> p t n", t=2)])
    all_done = [x_ for g in q_tiles for x_ in done[g]]
    prod.free = [all_done, all_done]
    res = []
    for c in range(2):
        w, landed = ws.take()
        for g in q_tiles[::2]:
            i, ps, t = project(w, landed, (g, g + 1), ready)
            bi, buf, bfree = prod.take()
            gate = mod[:, g // 2, 2:3, c * 512:(c + 1) * 512].to_broadcast([P, 2, 512])
            e = dve.do(tt(buf, ps[:, :, :], gate, ALU.mult), t, made, bfree)
            st.ps.done(i, e)
            for j in range(2):
                xv = xs[g + j][:, c * 512:(c + 1) * 512]
                e = dve.do(tt(xv, xv, buf[:, j, :], ALU.add), e)
            prod.done(bi, e)
            res.append(e)
        ws.done(t)

    made = []
    modulation(6, 1, res)
    ready = norm_modulate(q_tiles, res)
    SC = sb["SC"]
    n = len(q_tiles) * P
    qb = Turns([sb["bufs3"][:, 0:512], sb["bufs3"][:, 512:1024], sb["bufs3"][:, 1024:1536]])
    qb.free = [all_done] * 3
    for c in range(4):
        w, landed = ws.take()
        for b in range(4):
            blk = 4 * c + b
            i, ps, free = st.ps.take()
            t = pe.do(mm_group([(ps[:, 0, 0:n], [(w[:, k, b * P:(b + 1) * P], hT[:, k, 0:n]) for k in range(KT)])]), landed, ready, free)
            bi, buf, bfree = qb.take()
            e = act.do(af(buf[:, 0:n], ps[:, 0, 0:n], ACT.Copy), t, bfree)
            s_ = pe.do(mm_group([(ps[:, 1, g * P:(g + 1) * P], [(buf[:, g * P:(g + 1) * P], sub[:, 2 + blk % 2, :])]) for g in q_tiles]), e, have_sub)
            qb.done(bi, s_)
            f = dve.do(cp(SC[:, 0:len(q_tiles) * PH, :].rearrange("p (g h) n -> p g h n", h=PH)[:, :, blk // 2, (blk % 2) * P:(blk % 2 + 1) * P],
                          ps[:, 1, 0:n].rearrange("p (g n) -> p g n", n=P)), s_, have_QT, all_done)
            st.ps.done(i, e, f)
        ws.done(t)
    dve.do(lambda e: e.memset(sb["PO"][:, :, :], 0.0), all_done)


def routing(queue, rt, C, scores, after, idx, g):
    dve, act = queue.dve, queue.act
    v, ix, cand, cand2, tv, tp, abu, abf, ixf, eq, pick = (rt[n] for n in ("v", "ix", "cand", "cand2", "tv", "tp", "abu", "abf", "ixf", "eq", "pick"))

    def top16(vals, idxs, a, b, t):
        x = dve.do(lambda e: e.max(vals[:, 0:8], a), t)
        dve.do(lambda e: e.max_index(idxs[:, 0:8], vals[:, 0:8], a), x)
        x = dve.do(lambda e: e.match_replace(b, vals[:, 0:8], a, -3.0e38), x)
        x = dve.do(lambda e: e.max(vals[:, 8:16], b), x)
        return dve.do(lambda e: e.max_index(idxs[:, 8:16], vals[:, 8:16], b), x)

    t = after
    for half in range(2):
        t = top16(v[:, half, :], ix[:, half, :], scores[:, half * NK:(half + 1) * NK], cand2[:, 0:NK], t)
    copied = t
    sums = cand[:, :].rearrange("p (a b) -> p a b", a=TOPK)
    t = dve.do(tt(sums, wide(v[:, 0, :], [P, TOPK, TOPK], 2), wide(v[:, 1, :], [P, TOPK, TOPK], 1), ALU.add), t)
    t = top16(tv, tp, cand, cand2, t)
    m = dve.do(ts(rt["nm"], tv[:, 0:1], -1.0, None, ALU.mult), t)
    ex = act.do(af(rt["ex"], tv, ACT.Exp, bias=rt["nm"], acc=rt["z"]), m)
    dve.do(lambda e: e.tensor_scalar(abu[:, 0, :], tp, 4, None, ALU.logical_shift_right), t)
    t = dve.do(lambda e: e.tensor_scalar(abu[:, 1, :], tp, TOPK - 1, None, ALU.bitwise_and), t)
    t = dve.do(cp(abf, abu), t)
    t2 = dve.do(cp(ixf, ix), copied)
    iota = C("iota")
    for half in range(2):
        q = dve.do(tt(eq[:, half], wide(abf[:, half, :], [P, TOPK, TOPK], 2), wide(iota, [P, TOPK, TOPK], 1), ALU.is_equal), t)
        q = dve.do(tt(eq[:, half], eq[:, half], wide(ixf[:, half, :], [P, TOPK, TOPK], 1), ALU.mult), q, t2)
    t = dve.do(red(pick.rearrange("p a k -> p (a k)"), eq.rearrange("p a k j -> p (a k) j"), ALU.add), q)
    made = dve.do(stt(idx, pick[:, 0, :], float(NK), pick[:, 1, :], ALU.mult, ALU.add), t)
    r = dve.do(lambda e: e.reciprocal(rt["z"], rt["z"]), ex)
    dve.do(ts(g, rt["ex"], rt["z"], None, ALU.mult), r)
    return made


ALL = 1 << 20


class LoopLane(Lane):

    def waits(self, after):
        flatten, todo = [], list(after)
        while todo:
            a = todo.pop(0)
            if isinstance(a, list):
                todo = a + todo
            elif a is not None:
                flatten.append(a)
        best = {}
        for a in flatten:
            key = (id(a[0]), len(a) == 3)
            if self.seen.get(key, 0) < a[1] and (key not in best or best[key][1] < a[1]):
                best[key] = a
        now = {key[0] for key in [*self.seen, *best] if not key[1]}
        best = {key: a for key, a in best.items() if not (key[1] and key[0] in now)}
        for key, a in best.items():
            self.seen[key] = a[1]
        return list(best.values())

    def play_turn(self, e, f, per_turn, go):
        for fn, waits, sem, by in self.steps:
            values = [e.to_reg(f * per_turn[id(w[0])][0] + min(w[1], per_turn[id(w[0])][0])
                             + (per_turn[id(w[0])][1] if len(w) == 2 else 0)) for w in waits]
            if waits:
                e.wait_ge(go, 1)
            for w, v in zip(waits, values):
                e.wait_ge(w[0], v)
            fn(e).then_inc(sem, by)


def weights(st, rt, g, *after):
    dve, act = st.dve, st.act
    dots, w, z1, z2 = rt["dots"], rt["w"], rt["z1"], rt["z2"]
    t = dve.do(tt(z1, dots, dots, ALU.mult), *after)
    t = dve.do(ts(z1, z1, GELU_C * 0.044715, GELU_C, ALU.mult, ALU.add), t)
    t = dve.do(tt(z1, z1, dots, ALU.mult), t)
    t = dve.do(ts(z1, z1, -EXP_MAX, None, ALU.max), t)
    t = act.do(af(z2, z1, ACT.Exp, scale=-1.0), t)
    t = dve.do(ts(z2, z2, 1.0, None, ALU.add), t)
    t = dve.do(lambda e: e.reciprocal(z2, z2), t)
    t = dve.do(tt(w, dots, z2, ALU.mult), t)
    return dve.do(tt(w, w, g, ALU.mult), t)


def gather_row(ring_slot, tab, idx, k, layer):
    return lambda e: e.indirect_dma_start(out=ring_slot, out_offset=None, in_=tab,
                                          in_offset=bass.IndirectOffsetOnAxis(ap=idx[:, k:k + 1], axis=0),
                                          element_offset=layer * NE * D)


def dot_with(slot, h, out):
    return lambda e: e.scalar_tensor_tensor(out=slot, in0=slot, scalar=1.0, in1=h(), op0=ALU.mult, op1=ALU.mult, accum_out=out)


def first_head(st, sb, A, C, layer):
    rt, ring, SC = sb["rt"], sb["gring"], sb["SC"]
    u_tab = A["peer_u_2"].rearrange("l e d -> (l e) d")
    made = routing(st, rt, C, SC[:, 0, :], None, rt["idx"][:, 0, :], rt["g"][:, 0, :])
    for k in range(TOPK):
        c = st.count()
        c.n = 16
        st.soft.append(c)
        st.pool.steps.append((gather_row(ring[:, k, :], u_tab, rt["idx"][:, 0, :], k, layer), st.pool.waits([made]), c.sem, 16))
    last = (st.dve.sem, st.dve.n)
    st.dve.do(lambda e: e.memset(sb["psum"][:, 0:2, :], 0.0))
    routing(st, rt, C, SC[:, 1, :], last, rt["idx"][:, 1, :], rt["g"][:, 1, :])
    for k in range(TOPK):
        st.dve.do(dot_with(ring[:, k, :], lambda: sb["H"][:, 0, :], rt["dots"][:, k:k + 1]), (st.soft[k].sem, 16))


def experts(nc, st, sb, A, C, layer, tiles):
    rt, ring, H, PO, SC = sb["rt"], sb["gring"], sb["H"], sb["PO"], sb["SC"]
    u_tab, v_tab = (A[n].rearrange("l e d -> (l e) d") for n in ("peer_u_2", "peer_v_2"))
    st.dve, st.act, st.pe, st.pool = (LoopLane(x.sem) for x in (st.dve, st.act, st.pe, st.pool))
    dve, act, pe, pool = st.dve, st.act, st.pe, st.pool
    go = st.sem()
    NS = TOPK // 2
    u_slot, v_slot = [ring[:, j, :] for j in range(NS)], [ring[:, NS + j, :] for j in range(NS)]
    u_in, v_in = [st.count() for _ in range(NS)], [st.count() for _ in range(NS)]
    acc = sb["psum"][:, 0:2, :]
    cur = {}
    at_tile = lambda buf, g: buf[:, bass.DynSlice(cur[g], 1), :].rearrange("p o n -> p (o n)")
    as_acc = lambda ap: ap.rearrange("p (b n) -> p b n", b=2)

    def add(k):
        def fn(e):
            for half in range(2):
                last = e.matmul(acc[:, half, :], rt["diag"][:, k, :], v_slot[k % NS][:, half * 512:(half + 1) * 512],
                                start=(k == 0), stop=(k == TOPK - 1))
            return last
        return fn

    size = {}
    for part in range(2):
        start = {id(x): x.n for x in (dve, act, pe, pool)}
        here = lambda lane, n: (lane.sem, start[id(lane)] + n)
        if part == 0:
            before = lambda lane, n: (lane.sem, ALL, "before") if n is None else (lane.sem, size[id(lane)] + n, "before")
            size[id(pe)] = TOPK
        else:
            before = lambda lane, n: (lane.sem, size[id(lane)] if n is None else n)
        idx, g, v_idx = rt["idx"][:, part, :], rt["g"][:, part, :], rt["v_idx"][:, part, :]
        next_idx = rt["idx"][:, 1 - part, :]
        kept = dve.do(cp(v_idx, idx), before(dve, None))
        t = weights(st, rt, g, before(dve, None))
        have_w = dve.do(tt(rt["diag"], wide(C("ident"), [P, TOPK, P], 1), wide(rt["w"], [P, TOPK, P], 2), ALU.mult), t, before(pe, TOPK))
        tile = "g_before" if part == 0 else "g"
        taken = dve.do((lambda q: lambda e: e.tensor_tensor(as_acc(at_tile(PO, q)), as_acc(at_tile(PO, q)), acc, ALU.add))(tile), before(pe, TOPK))
        staged = act.do((lambda q: lambda e: e.copy(rt["scores"], SC[:, bass.DynSlice(cur[q], 1), :].rearrange("p o n -> p (o n)")))(f"f_routed{part}"),
                        before(dve, None))
        made = routing(st, rt, C, rt["scores"], staged, idx, g)
        route_step = made[1] - start[id(dve)]
        dot0 = dve.n - start[id(dve)]
        tile = "g" if part == 0 else "g_after"
        for k in range(TOPK):
            dve.do(dot_with(u_slot[k % NS], (lambda q: lambda: at_tile(H, q))(tile), rt["dots"][:, k:k + 1]),
                   have_w, (u_in[k % NS].sem, 32 * part + 16 * (k // NS) + 16))
        size[id(dve)], size[id(act)] = dve.n - start[id(dve)], act.n - start[id(act)]
        for k in range(TOPK):
            pe.do(add(k), have_w, taken, (v_in[k % NS].sem, 32 * part + 16 * (k // NS) + 16))
        for k in range(TOPK):
            dotted = before(dve, dot0 + k + NS + 1) if k < NS else here(dve, dot0 + k - NS + 1)
            added = before(pe, k + NS + 1) if k < NS else here(pe, k - NS + 1)
            for fn, count, after in (
                (gather_row(u_slot[k % NS], u_tab, next_idx, k, layer), u_in[k % NS], [before(dve, route_step), dotted]),
                (gather_row(v_slot[k % NS], v_tab, v_idx, k, layer), v_in[k % NS], [kept, added]),
            ):
                count.n += 16
                pool.steps.append((fn, pool.waits(after), count.sem, 16))
    per_turn = {id(x.sem): (x.n, x.n) for x in (dve, act, pe, pool)}
    per_turn |= {id(s.sem): (s.n, 0) for s in u_in + v_in}

    def play(lane):
        def fn(e):
            if lane.n:
                e.sem_inc(lane.sem, lane.n)
            e.sem_inc(go, 1)
            with e.Fori(0, tiles) as g:
                with e.Fori(0, PH // 2) as pair:
                    turn = g * (PH // 2) + pair
                    cur["g"], cur["g_before"] = g, ((turn + 4 * tiles - 1) >> 2) & (tiles - 1)
                    cur["g_after"] = ((turn + 1) >> 2) & (tiles - 1)
                    cur["f_routed0"], cur["f_routed1"] = ((turn * 2 + 2 + q) & (tiles * PH - 1) for q in range(2))
                    lane.play_turn(e, turn, per_turn, go)
            if lane is dve:
                total = per_turn[id(pe.sem)][0] * (tiles * PH // 2 + 1)
                e.wait_ge(pe.sem, total)
                e.wait_ge(dve.sem, per_turn[id(dve.sem)][0] * (tiles * PH // 2 + 1))
                e.tensor_tensor(as_acc(PO[:, tiles - 1, :]), as_acc(PO[:, tiles - 1, :]), acc, ALU.add).then_inc(dve.sem, 1)
            if lane is pool:
                for s in u_in + v_in:
                    e.wait_ge(s.sem, s.n * tiles * (PH // 2))
                e.dma_reset()
        return fn
    with nc.Block() as block:
        block.scalar(play(act))
        block.vector(play(dve))
        block.gpsimd(play(pool))
        block.tensor(play(pe))
    nc.all_engine_barrier(sems_to_clear=range(st.sems[0].num, st.sems[st.used - 1].num + 1))


def build(nc, A, out, upto=99):
    with ExitStack() as ctx:
        mem = Memory(nc, ctx)
        sems = [ctx.enter_context(nc.semaphore(f"count{i}")) for i in range(44)]
        psum = ctx.enter_context(nc.psum_tensor("psum", [P, 8, 512], F32))
        consts = mem("consts", [P, CONSTS.shape[1]])
        C = lambda name: consts[:, CONST_COLS[name][0]:CONST_COLS[name][0] + CONST_COLS[name][1]]
        x = mem("x", [P, NT, D])

        st = Stage(nc, sems, psum)
        c = st.count()
        st.sp.dma(c, consts[:, :], A["consts"])
        t = st.sp.dma(c, x[:, :, :], A["x"].rearrange("o (t p) d -> p (o t) d", p=P))
        st.sp.do(lambda e: e.nop(), t)
        st.run()

        with ExitStack() as block_memory:
            m1 = Memory(nc, block_memory)
            sb = {}
            for name, shape in (("hn", [P, NT, D]), ("hT", [P, KT, S]), ("QKp", [P, KT, S + 3]), ("qk", [P, KT, S]), ("arena", [P, 8192]),
                                ("v_aug", [P, NT, MH, MD + 1]), ("og", [P, NT, MW]), ("N", [P, NT, NAT]), ("sq", [P, NT * NG * HD]),
                                ("attn", [P, 6144]), ("small", [P, 640]), ("rows", [8, D]), ("pe_rows", [32, P]), ("g6", [P, 6, HD]),
                                ("cw2", [P, 2, HD]), ("cols", [P, KT, 8]), ("W0", [P, MH, S]), ("W1", [P, MH, P]),
                                ("cb", [P, 2 * 16 * NC_CMP]), ("kv", [16, 4 * HD])):
                sb[name] = m1(name, shape)
            ring = [m1(f"ring{i}", [P, 4096]) for i in range(3)]
            with nc.Fori(0, DEPTH) as l:
                st = Stage(nc, sems, psum)
                first_block(st, sb, A, C, x, ring, l)
                st.run()

        if upto == 1:
            st = Stage(nc, sems, psum)
            c = st.count()
            t = st.sp.dma(c, out.rearrange("o (t p) d -> p (o t) d", p=P), x[:, :, :])
            st.sp.do(lambda e: e.nop(), t)
            st.run()
            return

        with ExitStack() as block_memory:
            m2 = Memory(nc, block_memory)
            sb = {"psum": psum}
            for name, shape in (("mod", [P, 2, 3, D]), ("H", [P, 4, D]), ("gring", [P, TOPK, D]), ("scores", [P, 11264]),
                                ("work", [P, 4608]), ("xc", [P, NT, D]), ("small2", [P, 128]), ("gains", [P, 2, D]),
                                ("crow", [8, 2, P]), ("qkg", [P, 2, HD2]), ("sub", [P, 4, P]), ("sink", [P, H2])):
                sb[name] = m2(name, shape)
            gflat = flat(sb["gring"][:, :, :], "p k n -> p (k n)")
            sb["ring"] = [gflat[:, 4096 * i:4096 * (i + 1)] for i in range(3)]
            sb["hT2"] = gflat[:, 12288:16384].rearrange("p (k n) -> p k n", k=KT)
            big, work = sb["scores"], sb["work"]
            sb["Y"] = big[:, 0:6144].rearrange("p (g n) -> p g n", g=4)
            sb["QT2"] = big[:, 6144:11264].rearrange("p (h n) -> p h n", h=10)
            at = 4 * PH * 2 * NK
            sb["SC"] = big[:, 0:at].rearrange("p (f n) -> p f n", n=2 * NK)
            sb["brow"] = big[0:2, at:at + 1536].rearrange("p (j n) -> p j n", j=3)
            sb["mrow"] = big[0:2, at + 1536:at + 2560].rearrange("p (j n) -> p j n", j=2)
            sb["bufs"], sb["bufs3"] = work[:, 0:3072], work[:, 3072:4608]
            sb["PO"] = work[:, 0:4096].rearrange("p (g n) -> p g n", g=4)
            rt = {"diag": flat(sb["gains"][:, :, :], "p a n -> p (a n)").rearrange("p (k n) -> p k n", k=TOPK)}
            for name, n in (("scores", 256), ("v", 32), ("ix", 32), ("cand", 256), ("cand2", 256), ("tv", 16), ("tp", 16), ("abu", 32), ("abf", 32),
                            ("ixf", 32), ("eq", 512), ("pick", 32), ("nm", 1), ("z", 1), ("ex", 16), ("idx", 32), ("v_idx", 32), ("g", 32), ("dots", 16), ("w", 16), ("z1", 16), ("z2", 16)):
                rt[name] = big[:, at:at + n]
                at += n
            for name in ("v", "ix", "abu", "abf", "ixf", "pick", "idx", "v_idx", "g"):
                rt[name] = rt[name].rearrange("p (a k) -> p a k", a=2)
            rt["eq"] = rt["eq"].rearrange("p (a k j) -> p a k j", a=2, j=TOPK)
            for name in ("ix", "tp", "abu", "idx", "v_idx"):
                rt[name] = rt[name].bitcast(U32)
            sb["rt"] = rt
            xs = [x[:, 0, :], x[:, 1, :], sb["xc"][:, 0, :], sb["xc"][:, 1, :]]

            st = Stage(nc, sems, psum)
            c = st.count()
            t = st.sp.dma(c, sb["xc"][:, :, :], A["ctx_2"].rearrange("o (t p) d -> p (o t) d", p=P))
            st.sp.do(lambda e: e.nop(), t)
            st.run()
            for layer in range(DEPTH):
                tiles = 2 if layer == DEPTH - 1 else 4
                st = Stage(nc, sems, psum)
                attention_block(st, sb, A, C, xs, layer)
                st.run()
                if upto == 2 + 2 * layer:
                    break
                st = Stage(nc, sems, psum)
                first_head(st, sb, A, C, layer)
                st.run()
                experts(nc, Stage(nc, sems, psum), sb, A, C, layer, tiles)
                st = Stage(nc, sems, psum)
                for g in range(tiles):
                    t = st.dve.do(tt(sb["PO"][:, g, :], sb["PO"][:, g, :], sb["mod"][:, g // 2, 2, :], ALU.mult))
                    t = st.dve.do(tt(xs[g], xs[g], sb["PO"][:, g, :], ALU.add), t)
                st.run()
                if upto == 3 + 2 * layer:
                    break

            st = Stage(nc, sems, psum)
            c = st.count()
            t = st.sp.dma(c, out.rearrange("o (t p) d -> p (o t) d", p=P), x[:, :, :])
            if upto < 99:
                t = st.sp.dma(c, A["dbg"].rearrange("(t p) d -> p t d", p=P), sb["xc"][:, :, :])
            st.sp.do(lambda e: e.nop(), t)
            st.run()


INPUTS = ["x", "w_in", "b_if", "conv_qk", "m_norm", "moba_qk_norm", "nsa_q_norm", "nsa_k_norm", "cmp_pe", "cmp_w1", "cmp_w2", "w_out",
          "norm_mix", "norm_ffn", "w_ff1", "w_ff2", "c_2", "ctx_2", "c_ctx_2", "ada_w_2", "ada_b_2", "norm1_gain_2", "norm2_gain_2",
          "w_qkv_2", "q_norm_gain_2", "k_norm_gain_2", "w_o_2", "attn_sinks_2", "peer_w_q_2", "peer_sub_keys_2", "peer_u_2", "peer_v_2"]


def kernel(**inputs):
    import concourse.bacc as bacc
    from concourse.bass_utils import run_bass_kernel_spmd

    nc = bacc.Bacc("TRN2", target_bir_lowering=False, num_devices=1)
    arrays = {name: np.ascontiguousarray(inputs[name]) for name in INPUTS}
    arrays["consts"] = CONSTS
    A = {name: nc.dram_tensor(f"in_{name}", a.shape, F32, kind="ExternalInput").ap() for name, a in arrays.items()}
    out = nc.dram_tensor("out", (1, S, D), F32, kind="ExternalOutput").ap()
    build(nc, A, out)
    r = run_bass_kernel_spmd(nc, [{f"in_{name}": a for name, a in arrays.items()}], core_ids=[0])
    return r.results[0]["out"]
```

```python
from contextlib import ExitStack

import numpy as np

import concourse.bass as bass
from concourse import mybir

P = 128
F32 = mybir.dt.float32
U32 = mybir.dt.uint32
ALU = mybir.AluOpType
ACT = mybir.ActivationFunctionType
AX = mybir.AxisListType.X

D = 1024
KT = D // P
S = 256
NT = S // P
DEPTH = 2
EPS = 1e-6
NEG = -1e30
EXP_MAX = 80.0

MW, MH, MD = 512, 4, 128
HD = 64
NG = 22
IF0 = 4 * MW
NAT0 = IF0 + 2 * MH
NAT = NG * HD + 12
D_IN = NAT0 + NAT
D_FF = 4 * D
NC_CMP = S // 16 - 1
CMP_H = 128

H2, KV2, HD2 = 8, 2, 128
N_MOD = 6
PH, TOPK, NK = 8, 16, 128
NE = NK * NK
COLUMN_US, STEP_US = 4 / 2400, 0.7
GELU_C = 2.0 * float(np.sqrt(2.0 / np.pi))

CONST_COLS = {}


def constant_table():
    parts = {}
    i = np.arange(P)
    parts["ident"] = np.eye(P)
    parts["caus"] = np.concatenate([np.zeros((P, P)), np.where(i[None, :] <= i[:, None], 0.0, NEG)], 1)
    parts["causT"] = np.where(i[:, None] <= i[None, :], 0.0, NEG)
    tq = np.arange(S).reshape(NT, P).T[:, :, None]
    seen = (np.arange(NC_CMP) * 16 + 31)[None, None, :] <= tq
    parts["cmp_add"] = np.where(seen, 0.0, NEG).reshape(P, -1)
    parts["cmp_on"] = np.where(seen, 1.0, 0.0).reshape(P, -1)
    pos = np.arange(S, dtype=np.float32)
    inv = np.exp(np.float32(-np.log(500000.0)) * np.arange(8, dtype=np.float32) * np.float32(2.0 / 16)).astype(np.float32)
    ang = (pos[:, None] * inv[None, :]).astype(np.float32)
    per_tile = lambda a: a.reshape(NT, P, -1).transpose(1, 0, 2).reshape(P, -1)
    parts["cos1"], parts["sin1"] = per_tile(np.cos(ang)), per_tile(np.sin(ang))
    half = HD2 // 2
    inv2 = (np.float32(10000.0) ** (-np.arange(0, half, 2, dtype=np.float32) / np.float32(half))).astype(np.float32)
    row = np.repeat(np.arange(S // 64), 64).astype(np.float32)
    col = np.tile(np.arange(64), S // 64).astype(np.float32)
    ang2 = np.concatenate([row[:, None] * inv2, col[:, None] * inv2], 1).astype(np.float32)
    parts["cos2"], parts["sin2"] = per_tile(np.cos(ang2)), per_tile(np.sin(ang2))
    near = np.abs(pos[:, None] - pos[None, :]) <= 128
    win = np.concatenate([np.where(near, 0.0, NEG), np.zeros((S, S))], 1)
    parts["win"] = per_tile(win)
    parts["iota"] = np.tile(np.arange(TOPK), (P, 1))
    sel = np.zeros((P, 4, P))
    for h in range(4):
        sel[h, h] = 1.0
    parts["sel"] = sel.reshape(P, -1)
    parts["ones"] = np.ones((P, S))
    parts["m05"] = np.full((P, 48), -0.5)
    at = 0
    for name, a in parts.items():
        CONST_COLS[name] = (at, a.shape[1])
        at += a.shape[1]
    return np.concatenate(list(parts.values()), 1).astype(np.float32)


CONSTS = constant_table()


class Lane:

    def __init__(self, sem):
        self.sem, self.n, self.steps, self.seen = sem, 0, [], {}

    def waits(self, after):
        need = {}
        todo = list(after)
        while todo:
            a = todo.pop()
            if a is None:
                continue
            if isinstance(a, list):
                todo += a
                continue
            sem, v = a
            key = id(sem)
            if self.seen.get(key, 0) < v and (key not in need or need[key][1] < v):
                need[key] = (sem, v)
        for key, (_, v) in need.items():
            self.seen[key] = v
        return list(need.values())

    def do(self, fn, *after):
        self.n += 1
        self.steps.append((fn, self.waits(after), self.sem, 1))
        return (self.sem, self.n)

    def dma(self, count, out, in_, *after, scattered=False):
        count.n += 16
        self.steps.append((lambda e: e.dma_start(out, in_, allow_slow_non_contiguous=scattered), self.waits(after), count.sem, 16))
        return (count.sem, count.n)

    def play(self, e):
        for fn, waits, sem, by in self.steps:
            for s, v in waits:
                e.wait_ge(s, v)
            fn(e).then_inc(sem, by)


class PacedLane(Lane):

    def __init__(self, sem):
        super().__init__(sem)
        self.beside, self.rate, self.due = None, 0.0, 0.0

    def do(self, fn, *after):
        done = super().do(fn, *after)
        self.due += self.rate * (fn.us + STEP_US)
        while self.beside is not None and self.due >= 1.0:
            self.due -= 1.0
            try:
                next(self.beside)
            except StopIteration:
                self.beside = None
        return done


class Count:
    def __init__(self, sem):
        self.sem, self.n = sem, 0


class Turns:

    def __init__(self, bufs):
        self.bufs, self.free, self.i = bufs, [[] for _ in bufs], 0

    def take(self):
        i = self.i % len(self.bufs)
        self.i += 1
        free, self.free[i] = self.free[i], None
        assert free is not None, "a buffer is taken before its last reader is known"
        return i, self.bufs[i], free

    def done(self, i, *counts):
        self.free[i] = list(counts)


class Stage:
    def __init__(self, nc, sems, psum):
        self.nc, self.sems, self.used = nc, sems, 0
        self.pe, self.dve, self.act = PacedLane(self.sem()), Lane(self.sem()), Lane(self.sem())
        self.pool, self.sp = Lane(self.sem()), Lane(self.sem())
        self.soft = []
        self.ps = Turns([psum[:, 2 * i:2 * i + 2, :] for i in range(4)])

    def sem(self):
        self.used += 1
        return self.sems[self.used - 1]

    def count(self):
        return Count(self.sem())

    def play_pool(self, e):
        self.pool.play(e)
        if self.soft:
            for c in self.soft:
                e.wait_ge(c.sem, c.n)
            e.dma_reset()

    def run(self):
        with self.nc.Block() as block:
            block.sync(lambda e: self.sp.play(e))
            block.scalar(lambda e: self.act.play(e))
            block.vector(lambda e: self.dve.play(e))
            block.gpsimd(self.play_pool)
            block.tensor(lambda e: self.pe.play(e))
        self.nc.all_engine_barrier(sems_to_clear=range(self.sems[0].num, self.sems[self.used - 1].num + 1))


class Stream:

    def __init__(self, st, ring, plan):
        self.st, self.ring, self.plan = st, ring, plan
        self.counts = [st.count() for _ in ring]
        self.short = st.count()
        if any(len(p) > 2 for p in plan):
            st.soft.append(self.short)
        self.loaded, self.asked, self.at = [], 0, 0
        for _ in ring:
            self.load()

    def load(self, *after):
        if self.asked < len(self.plan):
            i = self.asked % len(self.ring)
            view, *parts = self.plan[self.asked]
            dst = view(self.ring[i])
            if len(parts) == 1:
                landed = self.st.sp.dma(self.counts[i], dst, parts[0], *after)
            else:
                for j, src in enumerate(parts):
                    landed = self.st.pool.dma(self.short, dst[:, j], src, *after)
            self.loaded.append((dst, landed))
            self.asked += 1

    def take(self):
        self.at += 1
        return self.loaded[self.at - 1]

    def done(self, *counts):
        self.load(*counts)


def mm_group(pairs):
    def fn(e):
        last = None
        for out, terms in pairs:
            for i, (a, b) in enumerate(terms):
                last = e.matmul(out, a, b, start=(i == 0), stop=(i == len(terms) - 1))
        return last
    fn.us = sum(len(terms) * int(np.prod(terms[0][1].shape[1:])) for _, terms in pairs) * COLUMN_US
    return fn


def turned(items, ident):
    def fn(e):
        last = None
        for out, a in items:
            last = e.transpose(out, a, ident[0:a.shape[0], 0:a.shape[0]])
        return last
    fn.us = len(items) * P * COLUMN_US
    return fn


def ts(out, a, s1, s2, op0, op1=None):
    if op1 is None:
        return lambda e: e.tensor_scalar(out, a, s1, None, op0)
    return lambda e: e.tensor_scalar(out, a, s1, s2, op0, op1)


def tt(out, a, b, op):
    return lambda e: e.tensor_tensor(out, a, b, op)


def stt(out, a, s, b, op0, op1):
    return lambda e: e.scalar_tensor_tensor(out=out, in0=a, scalar=s, in1=b, op0=op0, op1=op1)


def red(out, a, op, negate=False):
    if negate:
        return lambda e: e.tensor_reduce(out, a, AX, op, negate=True)
    return lambda e: e.tensor_reduce(out, a, AX, op)


def cp(out, a):
    return lambda e: e.tensor_copy(out, a)


def af(out, a, func, bias=None, scale=1.0, acc=None):
    def fn(e):
        kw = {} if acc is None else {"accum_out": acc}
        if bias is not None:
            kw["bias"] = bias
        return e.activation(out, a, func, scale=scale, **kw)
    return fn


def flat(ap, pattern, **kw):
    return ap.rearrange(pattern, **kw)


def wide(ap, shape, *axes):
    for a in axes:
        ap = ap.unsqueeze(a)
    return ap.to_broadcast(shape)


class Memory:
    def __init__(self, nc, ctx, prefix=""):
        self.nc, self.ctx, self.prefix = nc, ctx, prefix

    def __call__(self, name, shape, dt=F32):
        return self.ctx.enter_context(self.nc.sbuf_tensor(f"sb_{self.prefix}{name}", shape, dt))


def rms_scale(st, out, ss, width, n, m05, *after):
    a = st.dve.do(ts(out, ss, 1.0 / width, EPS, ALU.mult, ALU.add), *after)
    return st.pool.do(tt(out, out, m05, ALU.pow), a)


def sigmoid_of(st, out, a, *after):
    t = st.dve.do(ts(out, a, -EXP_MAX, None, ALU.max), *after)
    t = st.act.do(af(out, out, ACT.Exp, scale=-1.0), t)
    t = st.dve.do(ts(out, out, 1.0, None, ALU.add), t)
    return st.dve.do(lambda e: e.reciprocal(out, out), t)


def first_block(st, sb, A, C, x, ring, l):
    pe, dve, act, pool, sp = st.pe, st.dve, st.act, st.pool, st.sp
    at = lambda name: A[name][bass.DynSlice(l, 1)]
    ident = C("ident")
    chunk = lambda w, c0, n: (lambda slot: slot[:, 0:KT * n].rearrange("p (k n) -> p k n", k=KT),
                              w.rearrange("o (k p) n -> p (o k) n", p=P)[:, :, c0:c0 + n])
    w_in, w_out, w1, w2 = at("w_in"), at("w_out"), at("w_ff1"), at("w_ff2")
    nat_w = [(NAT0 - 8, 476), (NAT0 - 8 + 476, 476), (NAT0 - 8 + 952, NAT + 8 - 952)]
    plan = [chunk(w_in, 0, 512), chunk(w_in, 512, 512), chunk(w_in, 1024, 512), chunk(w_in, 1536, 512)]
    plan += [chunk(w_in, a, n) for a, n in nat_w]
    plan += [(lambda slot: slot[:, :].rearrange("p (c j h) -> p c j h", c=2, j=16),
              *(at("cmp_w1").rearrange("o c (j q) h -> c q (o j) h", q=P)[c] for c in range(2)))]
    plan += [chunk(w_out, 512 * c, 512) for c in range(2)]
    plan += [chunk(w1, 512 * c, 512) for c in range(8)]
    plan += [(lambda slot: slot[:, :].rearrange("p (f n) -> p f n", f=4),
              w2.rearrange("o (c f p) n -> c p (o f) n", p=P, f=4)[c]) for c in range(8)]

    hn = sb["hn"]
    hT = sb["hT"]
    arena, attn, sq, N = sb["arena"], sb["attn"], sb["sq"], sb["N"]
    QKp = attn[:, 0:2072].rearrange("p (k n) -> p k n", k=KT)
    qk = attn[:, 2072:4120].rearrange("p (k n) -> p k n", k=KT)
    W1 = attn[:, 4120:4632].rearrange("p (h n) -> p h n", h=MH)
    v_aug = attn[:, 4632:5664].rearrange("p (t h d) -> p t h d", t=NT, h=MH)
    cb = attn[:, 5664:6144]
    QN = arena[:, 0:3072].rearrange("p (t s d) -> p t s d", t=NT, d=HD)
    QT = arena[:, 3072:6144].rearrange("p (s n) -> p s n", n=S)
    og = arena[:, 6144:7168].rearrange("p (t n) -> p t n", t=NT)
    W0 = arena[:, 7168:8192].rearrange("p (h n) -> p h n", h=MH)
    uT = arena[:, :].rearrange("p (f n) -> p f n", n=S)
    sig = sq[:, 0:2048]
    rows = N[0:8, :, :].rearrange("p t n -> p (t n)")[:, 0:D]
    small = sb["small"]
    at_small = [0]

    def sm(n, rows=P):
        a = at_small[0]
        at_small[0] += n
        return small[0:rows, a:a + n]

    par = st.count()
    for r, name, n in ((0, "conv_qk", 4), (4, "norm_mix", 1), (5, "norm_ffn", 1)):
        act.dma(par, rows[r:r + n, :], at(name).rearrange("o (a n) -> (o a) n", a=1) if n == 1 else at(name).rearrange("o a n -> (o a) n"))
    act.dma(par, rows[6:7, 0:MW], at("m_norm"))
    pe_rows = sb["pe_rows"]
    act.dma(par, pe_rows[0:32, :], at("cmp_pe").rearrange("o k (j two) d -> (o k j) (two d)", two=2))
    g6 = sb["g6"]
    act.dma(par, g6[:, 0:2, :], at("moba_qk_norm").rearrange("o a d -> o (a d)").to_broadcast([P, 2 * HD]).rearrange("p (a d) -> p a d", a=2))
    act.dma(par, g6[:, 2, :], at("nsa_q_norm").to_broadcast([P, HD]))
    act.dma(par, g6[:, 3:6, :], at("nsa_k_norm").rearrange("o a d -> o (a d)").to_broadcast([P, 3 * HD]).rearrange("p (a d) -> p a d", a=3))
    cw2 = sb["cw2"]
    act.dma(par, cw2[:, :, :], at("cmp_w2").rearrange("o k h d -> h (o k) d"))
    bif = sm(2, 4)
    have_par = act.dma(par, bif, at("b_if").rearrange("o (g h) -> h (o g)", g=2), scattered=True)
    ws = Stream(st, ring, plan)

    cols = sb["cols"]
    i, ps, free = st.ps.take()
    pc = ps[:, 0, 0:64].rearrange("p (k r) -> p k r", r=8)
    t = pe.do(turned([(pc[:, k, 0:7 if k < 4 else 6], rows[0:7 if k < 4 else 6, k * P:(k + 1) * P]) for k in range(KT)]
                     + [(ps[:, 0, 64:96], pe_rows[0:32, :])], ident), have_par, free)
    have_cols = dve.do(cp(cols[:, 0:4, 0:7], pc[:, 0:4, 0:7]), t)
    have_cols = dve.do(cp(cols[:, 4:8, 0:6], pc[:, 4:8, 0:6]), t)
    peT = sm(32)
    have_pe = dve.do(cp(peT, ps[:, 0, 64:96]), t)
    st.ps.done(i, have_pe)

    def norm_to_T(gain_col, *after):
        ss, rs = sm(NT), sm(NT)
        a = [act.do(af(hn[:, t, :], x[:, t, :], ACT.Square, acc=ss[:, t:t + 1]), *after) for t in range(NT)]
        r = rms_scale(st, rs, ss, D, NT, C("m05")[:, 0:NT], a)
        ready = []
        for t in range(NT):
            b = dve.do(ts(hn[:, t, :], x[:, t, :], rs[:, t:t + 1], None, ALU.mult), r)
            i, ps, free = st.ps.take()
            c = pe.do(turned([(ps[:, k // 4, (k % 4) * P:(k % 4 + 1) * P], hn[:, t, k * P:(k + 1) * P]) for k in range(KT)], ident), b, free)
            d = dve.do(tt(hT[:, :, t * P:(t + 1) * P], flat(ps, "p b (k n) -> p (b k) n", k=4),
                          wide(cols[:, :, gain_col:gain_col + 1], [P, KT, P]), ALU.mult), c, have_cols)
            st.ps.done(i, d)
            ready.append(d)
        return ready

    ready_h = norm_to_T(4)

    pad0 = dve.do(lambda e: e.memset(QKp[:, :, 0:3], 0.0))
    for c in range(2):
        w, landed = ws.take()
        last = []
        for half in range(2):
            i, ps, free = st.ps.take()
            t = pe.do(mm_group([(ps[:, 0, b * S:(b + 1) * S],
                                 [(w[:, k, (2 * half + b) * P:(2 * half + b + 1) * P], hT[:, k, :]) for k in range(KT)])
                                for b in range(2)]), landed, ready_h, free)
            blk = 4 * c + 2 * half
            e = act.do(af(QKp[:, blk:blk + 2, 3:3 + S], ps[:, 0, :].rearrange("p (b n) -> p b n", b=2), ACT.Copy), t)
            st.ps.done(i, e)
            last.append(e)
            for b in range(blk, blk + 2):
                y = dve.do(ts(qk[:, b, :], QKp[:, b, 0:S], cols[:, b, 0:1], None, ALU.mult), e, pad0, have_cols)
                for j in range(1, 4):
                    y = dve.do(stt(qk[:, b, :], QKp[:, b, j:j + S], cols[:, b, j:j + 1], qk[:, b, :], ALU.mult, ALU.add), y)
        ws.done(t)
    qkf = qk[:, :, :].rearrange("p b n -> p (b n)")
    t = sigmoid_of(st, sig, qkf, y)
    have_qk = dve.do(tt(qkf, qkf, sig, ALU.mult), t)

    def natural(out, w, landed, c0, n, off=0):
        i, ps, free = st.ps.take()
        t = pe.do(mm_group([(ps[:, t, 0:n], [(hT[:, k, t * P:(t + 1) * P], w[:, k, c0:c0 + n]) for k in range(KT)])
                            for t in range(NT)]), landed, ready_h, free)
        return i, ps, t

    w, landed = ws.take()
    i, ps, t = natural(None, w, landed, 0, MW)
    ones = dve.do(lambda e: e.memset(v_aug[:, :, :, MD:MD + 1], 1.0))
    have_v = act.do(af(v_aug[:, :, :, 0:MD], ps[:, :, :].rearrange("p t (h d) -> p t h d", h=MH), ACT.Copy), t)
    st.ps.done(i, have_v)
    ws.done(t)
    w, landed = ws.take()
    i, ps, t = natural(None, w, landed, 0, MW)
    t2 = dve.do(ts(og[:, :, :], ps[:, :, :], -EXP_MAX, None, ALU.max), t)
    st.ps.done(i, t2)
    ws.done(t)
    t2 = act.do(af(og[:, :, :], og[:, :, :], ACT.Exp, scale=-1.0), t2)
    t2 = dve.do(ts(og[:, :, :], og[:, :, :], 1.0, None, ALU.add), t2)
    have_og = dve.do(lambda e: e.reciprocal(og[:, :, :], og[:, :, :]), t2)

    w, landed = ws.take()
    gi, gps, free = st.ps.take()
    gates = pe.do(mm_group([(gps[0:MH, 0, g * S:(g + 1) * S], [(w[:, k, g * MH:(g + 1) * MH], hT[:, k, :]) for k in range(KT)])
                            for g in range(2)]), landed, ready_h, free)
    i, ps, t = natural(None, w, landed, 8, 468)
    e = act.do(af(N[:, :, 0:468], ps[:, :, 0:468], ACT.Copy), t)
    st.ps.done(i, e)
    ws.done(t)
    base = 468
    for c in range(2):
        w, landed = ws.take()
        n = nat_w[c + 1][1]
        i, ps, t = natural(None, w, landed, 0, n)
        have_N = act.do(af(N[:, :, base:base + n], ps[:, :, 0:n], ACT.Copy), t)
        st.ps.done(i, have_N)
        ws.done(t)
        base += n
    hT_free = t

    rI, rF, rA, rL, rB, rC, rM, rN = (sb["sq"][0:MH, j * S:(j + 1) * S] for j in range(8))
    t = dve.do(ts(rI, gps[0:MH, 0, 0:S], bif[:, 0:1], None, ALU.add), gates)
    f = dve.do(ts(rF, gps[0:MH, 0, S:2 * S], bif[:, 1:2], None, ALU.add), gates)
    st.ps.done(gi, t, f)
    t = dve.do(stt(rA, rF, -1.0, rF, ALU.mult, ALU.max), f)
    t = act.do(af(rA, rA, ACT.Exp, scale=-1.0), t)
    t = act.do(af(rL, rA, ACT.Ln, bias=1.0), t)
    t = dve.do(stt(rL, rF, 0.0, rL, ALU.min, ALU.subtract), t)
    t = dve.do(lambda e: e.tensor_tensor_scan(rB, C("ones")[0:MH, :], rL, 0.0, ALU.mult, ALU.add), t)
    t = dve.do(tt(rC, rI, rB, ALU.subtract), t)
    m = dve.do(lambda e: e.tensor_tensor_scan(rM, rC, rC, 0.0, ALU.max, ALU.max), t)
    n = dve.do(stt(rN, rB, -1.0, rM, ALU.mult, ALU.subtract), m)
    i, ps, free = st.ps.take()
    cn = ps[:, 0, 0:16].rearrange("p (a t h) -> p a t h", a=2, t=NT)
    t = pe.do(turned([(cn[:, a, t, :], (rC, rN)[a][:, t * P:(t + 1) * P]) for a in range(2) for t in range(NT)], ident), n, free)
    cc = sm(16).rearrange("p (a t h) -> p a t h", a=2, t=NT)
    have_cc = dve.do(cp(cc, cn), t)
    st.ps.done(i, have_cc)
    em = sm(8).rearrange("p (t h) -> p t h", t=NT)
    have_em = act.do(af(em, cc[:, 1], ACT.Exp), have_cc)
    bi, bps, free = st.ps.take()
    sel = C("sel").rearrange("p (h m) -> p h m", h=4)
    t = pe.do(mm_group([(bps[:, h // 2, (h % 2) * S:(h % 2 + 1) * S], [(sel[0:MH, h, :], rM)]) for h in range(MH)]), m, free)
    Mb = flat(bps, "p b (h n) -> p (b h) n", h=2)
    causT = wide(C("causT"), [P, MH, P], 1)
    a0 = dve.do(tt(W0[:, :, 0:P], causT, Mb[:, :, 0:P], ALU.subtract), t)
    a1 = dve.do(tt(W1[:, :, :], causT, Mb[:, :, P:S], ALU.subtract), t)
    for h in range(MH):
        w00 = act.do(af(W0[:, h, 0:P], W0[:, h, 0:P], ACT.Exp, bias=cc[:, 0, 0, h:h + 1]), a0, have_cc)
        w01 = act.do(af(W0[:, h, P:S], Mb[:, h, P:S], ACT.Exp, bias=cc[:, 0, 0, h:h + 1], scale=-1.0), a0, a1, have_cc)
        w11 = act.do(af(W1[:, h, :], W1[:, h, :], ACT.Exp, bias=cc[:, 0, 1, h:h + 1]), a1, have_cc)
    st.ps.done(bi, a0, a1, w01)
    i0, p0, free0 = st.ps.take()
    i1, p1, free1 = st.ps.take()
    s0 = flat(p0, "p b (h n) -> p (b h) n", h=2)
    s1 = p1[:, 0, :].rearrange("p (h n) -> p h n", h=MH)
    t0 = pe.do(mm_group([(s0[:, h, :], [(qk[:, MH + h, 0:P], qk[:, h, :])]) for h in range(MH)]), have_qk, free0)
    t1 = pe.do(mm_group([(s1[:, h, :], [(qk[:, MH + h, P:S], qk[:, h, P:S])]) for h in range(MH)]), have_qk, free1)
    u0 = dve.do(stt(W0[:, :, :], s0, MD ** -0.5, W0[:, :, :], ALU.mult, ALU.mult), t0, w01)
    u1 = dve.do(stt(W1[:, :, :], s1, MD ** -0.5, W1[:, :, :], ALU.mult, ALU.mult), t1, w11)
    st.ps.done(i0, u0)
    st.ps.done(i1, u1)
    dn = sm(8).rearrange("p (t h) -> p t h", t=NT)
    mix = hn
    for t in range(NT):
        i, ps, free = st.ps.take()
        o = lambda h: ps[:, h // 2, (h % 2) * (MD + 1):(h % 2 + 1) * (MD + 1)]
        if t == 0:
            terms = [(o(h), [(W0[:, h, 0:P], v_aug[:, 0, h, :])]) for h in range(MH)]
        else:
            terms = [(o(h), [(W0[:, h, P:S], v_aug[:, 0, h, :]), (W1[:, h, :], v_aug[:, 1, h, :])]) for h in range(MH)]
        a = pe.do(mm_group(terms), u0, u1, have_v, ones, free)
        view = ps[:, :, 0:2 * (MD + 1)].rearrange("p b (j c) -> p b j c", j=2)
        d4 = dn[:, t, :].rearrange("p (b j) -> p b j", b=2)
        b = dve.do(stt(d4, view[:, :, :, MD], -1.0, em[:, t, :].rearrange("p (b j) -> p b j", b=2), ALU.mult, ALU.max), a, have_em)
        b = dve.do(tt(d4, view[:, :, :, MD], d4, ALU.max), b)
        b = dve.do(lambda e, d4=d4: e.reciprocal(d4, d4), b)
        hm = dve.do(tt(mix[:, t, 0:MW].rearrange("p (b j d) -> p b j d", b=2, j=2), view[:, :, :, 0:MD],
                       wide(d4, [P, 2, 2, MD], 3), ALU.mult), b, hT_free)
        st.ps.done(i, hm)
    m4 = mix[:, :, 0:MW].rearrange("p t (h d) -> p t h d", h=MH)
    scr = sq[:, 0:NT * MW].rearrange("p (t n) -> p t n", t=NT)
    t = dve.do(tt(scr, mix[:, :, 0:MW], mix[:, :, 0:MW], ALU.mult), hm)
    ssm = sm(8)
    t = dve.do(red(ssm, sq[:, 0:NT * MW].rearrange("p (g d) -> p g d", d=MD), ALU.add), t)
    sq_free = t
    t = rms_scale(st, ssm, ssm, MD, 8, C("m05")[:, 0:8], t)
    t = dve.do(tt(m4, m4, wide(ssm.rearrange("p (t h) -> p t h", t=NT), [P, NT, MH, MD], 3), ALU.mult), t)
    mixed = [dve.do(tt(mix[:, :, 0:MW], mix[:, :, 0:MW], og[:, :, :], ALU.mult), t, have_og)]

    heads = N[:, :, 0:NG * HD].rearrange("p t (g d) -> p t g d", d=HD)
    sq4 = sq[:, :].rearrange("p (t n) -> p t n", t=NT)
    t = dve.do(tt(sq4, N[:, :, 0:NG * HD], N[:, :, 0:NG * HD], ALU.mult), have_N, sq_free)
    rs = sm(NT * NG)
    t = dve.do(red(rs, sq[:, :].rearrange("p (g d) -> p g d", d=HD), ALU.add), t)
    t = rms_scale(st, rs, rs, HD, NT * NG, C("m05")[:, 0:NT * NG], t)
    rs3 = rs.rearrange("p (t g) -> p t g", t=NT)
    t1 = dve.do(ts(rs3[:, :, 0:4], rs3[:, :, 0:4], HD ** -0.5, None, ALU.mult), t)
    t2 = dve.do(ts(rs3[:, :, 12:16], rs3[:, :, 12:16], HD ** -0.5, None, ALU.mult), t)
    sqh = sq[:, :].rearrange("p (t g d) -> p t g d", t=NT, d=HD)
    for tl in range(NT):
        t = dve.do(tt(sqh[:, tl], heads[:, tl], wide(rs3[:, tl], [P, NG, HD], 2), ALU.mult), t1, t2)
    for s0_, n_, g0_, gain in ((0, 4, 0, 0), (4, 4, 4, 1), (8, 4, 12, 2), (16, 4, 12, 2), (12, 2, 18, 4), (14, 2, 20, 5)):
        for tl in range(NT):
            src = sqh[:, tl, g0_:g0_ + n_, :] if n_ == 4 else sqh[:, tl, g0_:g0_ + 1, :].to_broadcast([P, 2, HD])
            slots = dve.do(tt(QN[:, tl, s0_:s0_ + n_, :], src, g6[:, gain:gain + 1, :].to_broadcast([P, n_, HD]), ALU.mult), t, have_par)
    for c in range(2):
        for tl in range(NT):
            slots = dve.do(cp(QN[:, tl, 20 + 2 * c:22 + 2 * c, :], heads[:, tl, 16 + c:17 + c, :].to_broadcast([P, 2, HD])), have_N)
    rope = attn[:, 0:1024].rearrange("p (a s d) -> p a s d", a=4, d=8)
    for tl in range(NT):
        cos = wide(C("cos1")[:, tl * 8:(tl + 1) * 8], [P, 16, 8], 1)
        sin = wide(C("sin1")[:, tl * 8:(tl + 1) * 8], [P, 16, 8], 1)
        x1, x2 = QN[:, tl, 0:16, 0:8], QN[:, tl, 0:16, 8:16]
        ra, rb, rc, rd = (attn[:, 512 * tl + 128 * j:512 * tl + 128 * (j + 1)].rearrange("p (s d) -> p s d", d=8) for j in range(4))
        dve.do(tt(ra, x1, cos, ALU.mult), slots)
        dve.do(tt(rb, x2, sin, ALU.mult), slots)
        dve.do(tt(rc, x2, cos, ALU.mult), slots)
        u = dve.do(tt(rd, x1, sin, ALU.mult), slots)
        dve.do(tt(x1, ra, rb, ALU.subtract), u)
        roped = dve.do(tt(x2, rc, rd, ALU.add), u)
    have_QT = []
    for q in range(6):
        i, ps, free = st.ps.take()
        a = pe.do(turned([(ps[:, b, t * P:(t + 1) * P], QN[:, t, 4 * q + 2 * b:4 * q + 2 * b + 2, :].rearrange("p s d -> p (s d)"))
                          for b in range(2) for t in range(NT)], ident), roped, free)
        b = act.do(af(QT[:, 2 * q:2 * q + 2, :], ps[:, :, 0:S], ACT.Copy), a)
        st.ps.done(i, b)
        have_QT.append(b)

    cb5 = cb[:, :].rearrange("p (c j n) -> p c j n", c=2, j=16)
    for c in range(2):
        for half in range(2):
            r = slice(64 * half, 64 * half + 64)
            tok = QT[r, 10 + c, :].rearrange("p (n q) -> p q n", q=16)
            for g in range(2):
                cbs = dve.do(tt(cb5[r, c, 8 * g:8 * g + 8, :], tok[:, half::2, g:g + NC_CMP],
                                wide(peT[r, 16 * c + 8 * g:16 * c + 8 * g + 8], [64, 8, NC_CMP], 2), ALU.add), have_QT, have_pe)
    w, landed = ws.take()
    i, ps, free = st.ps.take()
    t = pe.do(mm_group([(ps[:, 0, 16 * c:16 * c + NC_CMP], [(w[:, c, j, :], cb5[:, c, j, :]) for j in range(16)]) for c in range(2)]), cbs, landed, free)
    hidden = t
    ws.done(t)
    hid = sm(32).rearrange("p (c n) -> p c n", c=2)[:, :, 0:NC_CMP]
    sg = sm(32).rearrange("p (c n) -> p c n", c=2)[:, :, 0:NC_CMP]
    t = act.do(af(hid, ps[:, 0, 0:32].rearrange("p (c n) -> p c n", c=2)[:, :, 0:NC_CMP], ACT.Copy), t)
    st.ps.done(i, t)
    t = sigmoid_of(st, sg, hid, t)
    t = dve.do(tt(hid, hid, sg, ALU.mult), t)
    i, ps, free = st.ps.take()
    t = pe.do(mm_group([(ps[0:NC_CMP, 0, c * HD:(c + 1) * HD], [(hid[:, c, :], cw2[:, c, :])]) for c in range(2)]), t, have_par, free)
    kv = sb["kv"]
    kcn, vcn, ksq = kv[0:NC_CMP, 0:HD], kv[0:NC_CMP, HD:2 * HD], kv[0:NC_CMP, 2 * HD:4 * HD]
    t = dve.do(cp(kv[0:NC_CMP, 0:2 * HD], ps[0:NC_CMP, 0, 0:2 * HD]), t)
    have_vc = t
    st.ps.done(i, t)
    kss = sm(1)[0:NC_CMP]
    t = dve.do(tt(ksq[:, 0:HD], kcn, kcn, ALU.mult), t)
    t = dve.do(red(kss, ksq[:, 0:HD], ALU.add), t)
    t = rms_scale(st, kss, kss, HD, 1, C("m05")[0:NC_CMP, 0:1], t)
    t = dve.do(stt(ksq[:, 0:HD], kcn, kss, g6[0:NC_CMP, 3, :], ALU.mult, ALU.mult), t)
    t = dve.do(cp(ksq[:, HD:2 * HD], ksq[:, 0:HD]), t)
    i, ps, free = st.ps.take()
    t = pe.do(turned([(ps[:, 0, 0:NC_CMP], ksq)], ident), t, free)
    kcT = sm(16)
    t = dve.do(cp(kcT[:, 0:NC_CMP], ps[:, 0, 0:NC_CMP]), t)
    st.ps.done(i, t)
    half_of = lambda h: slice(64 * (h % 2), 64 * (h % 2) + 64)
    i, ps, free = st.ps.take()
    sc = ps[:, :, 0:64].rearrange("p b (t j n) -> p b t j n", t=NT, j=2)
    t = pe.do(mm_group([(sc[:, h % 2, t, h // 2, 0:NC_CMP], [(QT[half_of(h), 8 + h // 2, t * P:(t + 1) * P], kcT[half_of(h), 0:NC_CMP])])
                        for t in range(NT) for h in range(4)]), t, have_QT, free)
    pcb = sm(8 * NC_CMP)
    pc5 = pcb.rearrange("p (b t j n) -> p b t j n", b=2, t=NT, j=2)
    pc3 = pcb.rearrange("p (g n) -> p g n", g=8)
    per_t = lambda name: wide(C(name).rearrange("p (t n) -> p t n", t=NT), [P, NT, 2, NC_CMP], 2)
    s1 = dve.do(tt(pc5[:, 0], sc[:, 0, :, :, 0:NC_CMP], per_t("cmp_add"), ALU.add), t)
    t = dve.do(tt(pc5[:, 1], sc[:, 1, :, :, 0:NC_CMP], per_t("cmp_add"), ALU.add), t)
    st.ps.done(i, t)
    cm, cs = sm(8), sm(8)
    t = dve.do(red(cm, pc3, ALU.max), t)
    t = dve.do(tt(pc3, pc3, wide(cm, [P, 8, NC_CMP], 2), ALU.subtract), t)
    t = act.do(af(pcb, pcb, ACT.Exp), t)
    t = dve.do(red(cs, pc3, ALU.add), t)
    t = dve.do(lambda e: e.reciprocal(cs, cs), t)
    t = dve.do(tt(pc3, pc3, wide(cs, [P, 8, NC_CMP], 2), ALU.mult), t)
    t1 = dve.do(tt(pc5[:, 0], pc5[:, 0], per_t("cmp_on"), ALU.mult), t)
    t = dve.do(tt(pc5[:, 1], pc5[:, 1], per_t("cmp_on"), ALU.mult), t)
    i, ps, free = st.ps.take()
    t = pe.do(turned([(ps[0:NC_CMP, g // 4, (g % 4) * P:(g % 4 + 1) * P], pc3[:, g, :]) for g in range(8)], ident), t, free)
    pcT = sq[0:NC_CMP, 0:1024]
    t = act.do(af(pcT.rearrange("p (b n) -> p b n", b=2), ps[0:NC_CMP, :, :], ACT.Copy), t, slots)
    st.ps.done(i, t)
    i, ps, free = st.ps.take()
    t = pe.do(mm_group([(ps[:, 0, (4 * tl + 2 * j + b) * HD:(4 * tl + 2 * j + b + 1) * HD],
                         [(pcT[:, (4 * b + 2 * tl + j) * P:(4 * b + 2 * tl + j + 1) * P], vcn)]) for b in range(2) for tl in range(NT) for j in range(2)]), t, have_vc, free)
    gt = sm(24).rearrange("p (t g) -> p t g", t=NT)
    g1 = sigmoid_of(st, gt, N[:, :, NG * HD:NG * HD + 12], have_N)
    gate = lambda t, b: wide(gt[:, t, 4 * b:4 * b + 4], [P, 4, HD], 2)
    yn = lambda t: mix[:, t, 768:1024].rearrange("p (h d) -> p h d", h=4)
    for tl in range(NT):
        have_oc = dve.do(tt(yn(tl), ps[:, 0, tl * S:(tl + 1) * S].rearrange("p (h d) -> p h d", h=4), gate(tl, 0), ALU.mult), t, g1, hT_free)
    st.ps.done(i, have_oc)

    bufs = Turns([attn[:, 0:3072], attn[:, 3072:6144]])
    bufs.free = [[roped, mixed[0], hidden], [roped, mixed[0], hidden]]
    tmp = sq[:, 1024:1024 + S].rearrange("p (h d) -> p h d", h=4)
    stat = sm(2 * 8)
    for f, (q0, k0, v_of) in enumerate(((0, lambda h: 2 + h // 2, lambda h: 8 + h), (4, lambda h: 6, lambda h: 19), (4, lambda h: 7, lambda h: 21))):
        for t in range(NT):
            nk = P * (t + 1)
            bi, buf, bfree = bufs.take()
            sc, pT = buf[:, 0:4 * nk].rearrange("p (h n) -> p h n", h=4), buf[:, 1024:1024 + 4 * nk]
            pr = buf[:, 2048:2048 + 4 * nk].rearrange("p (h n) -> p h n", h=4)
            mx, den = stat[:, 8 * bi:8 * bi + 4], stat[:, 8 * bi + 4:8 * bi + 8]
            i, ps, free = st.ps.take()
            s_of = flat(ps, "p b (h n) -> p (b h) n", h=2)[:, :, 0:nk]
            a = pe.do(mm_group([(s_of[:, 2 * (h % 2) + h // 2, :], [(QT[half_of(h), q0 + h // 2, t * P:(t + 1) * P], QT[half_of(h), k0(h), 0:nk])])
                                for h in range(4)]), have_QT, free)
            a = dve.do(tt(sc, s_of, wide(C("caus")[:, S - nk:S], [P, 4, nk], 1), ALU.add), a, bfree)
            st.ps.done(i, a)
            a = dve.do(red(mx, sc, ALU.max, negate=True), a)
            for g in range(4):
                h = 2 * (g % 2) + g // 2
                b = act.do(af(pr[:, g, :], sc[:, g, :], ACT.Exp, bias=mx[:, g:g + 1], acc=den[:, h:h + 1]), a, bfree)
            r = dve.do(lambda e, den=den: e.reciprocal(den, den), b)
            i, ps, free = st.ps.take()
            nb = 4 * (t + 1)
            c = pe.do(turned([(ps[:, j // 4, (j % 4) * P:(j % 4 + 1) * P], pr[:, j // (t + 1), (j % (t + 1)) * P:(j % (t + 1) + 1) * P])
                              for j in range(nb)], ident), b, free)
            c2 = act.do(af(pT.rearrange("p (b n) -> p b n", n=512), ps[:, 0:t + 1, :], ACT.Copy), c, bfree)
            st.ps.done(i, c2)
            i, ps, free = st.ps.take()
            d = pe.do(mm_group([(ps[:, 0, h * HD:(h + 1) * HD],
                                 [(pT[:, ((2 * (h % 2) + h // 2) * (t + 1) + kt) * P:((2 * (h % 2) + h // 2) * (t + 1) + kt + 1) * P], heads[:, kt, v_of(h), :]) for kt in range(t + 1)])
                                for h in range(4)]), c2, free)
            o = ps[:, 0, 0:S].rearrange("p (h d) -> p h d", h=4)
            if f == 0:
                e = dve.do(tt(mix[:, t, 512:768].rearrange("p (h d) -> p h d", h=4), o, wide(den, [P, 4, HD], 2), ALU.mult), d, r, hT_free)
            else:
                e = dve.do(tt(tmp, o, wide(den, [P, 4, HD], 2), ALU.mult), d, r)
                g = dve.do(tt(tmp, tmp, gate(t, f), ALU.mult), e)
                g = dve.do(tt(yn(t), yn(t), tmp, ALU.add), g, have_oc)
                mixed.append(g)
            st.ps.done(i, e)
            bufs.done(bi, e)
            mixed.append(e)

    ready = []
    for t in range(NT):
        i, ps, free = st.ps.take()
        c = pe.do(turned([(ps[:, k // 4, (k % 4) * P:(k % 4 + 1) * P], mix[:, t, k * P:(k + 1) * P]) for k in range(KT)], ident), mixed, free)
        d = dve.do(tt(hT[:, 0:4, t * P:(t + 1) * P], ps[:, 0, :].rearrange("p (k n) -> p k n", k=4),
                      wide(cols[:, 0:4, 6:7], [P, 4, P]), ALU.mult), c)
        d2 = act.do(af(hT[:, 4:8, t * P:(t + 1) * P], ps[:, 1, :].rearrange("p (k n) -> p k n", k=4), ACT.Copy), c)
        st.ps.done(i, d, d2)
        ready += [d, d2]
    ready_h = ready
    for c in range(2):
        w, landed = ws.take()
        i, ps, t = natural(None, w, landed, 0, 512)
        ws.done(t)
        xv = x[:, :, c * 512:(c + 1) * 512]
        added = dve.do(tt(xv, xv, ps[:, :, :], ALU.add), t, ready)
        st.ps.done(i, added)

    ready_h = norm_to_T(5, added)
    rl = Turns([attn[:, 0:1024], attn[:, 1024:2048]])
    squared = []
    for c in range(8):
        w, landed = ws.take()
        i, ps, free = st.ps.take()
        t = pe.do(mm_group([(ps[:, b // 2, (b % 2) * S:(b % 2 + 1) * S],
                             [(w[:, k, b * P:(b + 1) * P], hT[:, k, :]) for k in range(KT)]) for b in range(4)]), landed, ready_h, free)
        ws.done(t)
        ri, rbuf, rfree = rl.take()
        a = act.do(af(rbuf.rearrange("p (b n) -> p b n", b=2), ps[:, :, :], ACT.Relu), t, rfree)
        st.ps.done(i, a)
        b = dve.do(tt(uT[:, 4 * c:4 * c + 4, :].rearrange("p f n -> p (f n)"), rbuf, rbuf, ALU.mult), a)
        rl.done(ri, b)
        squared.append(b)
    (i0, p0, f0), (i1, p1, f1) = st.ps.take(), st.ps.take()
    acc = (p0, p1)
    for c in range(8):
        w, landed = ws.take()

        def fn(e, c=c, w=w):
            for f in range(4):
                for t in range(NT):
                    for half in range(2):
                        last = e.matmul(acc[t][:, half, :], uT[:, 4 * c + f, t * P:(t + 1) * P], w[:, f, half * 512:(half + 1) * 512],
                                        start=(c == 0 and f == 0), stop=(c == 7 and f == 3))
            return last
        fn.us = 4 * NT * D * COLUMN_US
        t = pe.do(fn, squared[c], landed, f0, f1)
        ws.done(t)
    for tl in range(NT):
        xv = x[:, tl, :].rearrange("p (b n) -> p b n", b=2)
        fin = dve.do(tt(xv, xv, acc[tl][:, :, :], ALU.add), t)
    return fin



def in_turn(steps, width):
    waiting, running = list(steps), []
    while waiting or running:
        while waiting and len(running) < width:
            running.append(waiting.pop(0))
        for g in list(running):
            try:
                next(g)
            except StopIteration:
                running.remove(g)


def attention_block(st, sb, A, C, xs, kept, layer, part):
    pe, dve, act, pool, sp = st.pe, st.dve, st.act, st.pool, st.sp
    context, latents, last = part == "context", part == "latents", part == "last"
    ident, sel = C("ident"), C("sel").rearrange("p (h m) -> p h m", h=4)
    chunk = lambda w, c: (lambda slot: slot[:, :].rearrange("p (k n) -> p k n", k=KT),
                          w.rearrange("(k p) n -> p k n", p=P)[:, :, c * 512:(c + 1) * 512])
    ada, wqkv, wo, wq = A["ada_w_2"][layer], A["w_qkv_2"][layer], A["w_o_2"][layer], A["peer_w_q_2"][layer]
    ada_chunks = [chunk(ada, c) for c in range(12)] if not latents else []
    plan = ada_chunks[:6] + [chunk(wqkv, c) for c in range(3)] + [chunk(wo, c) for c in range(2)]
    plan += ada_chunks[6:] + [chunk(wq, c) for c in range(4)]
    q_tiles = [2, 3] if context else [0, 1]
    h_tiles = [0, 1, 2, 3] if last else q_tiles
    mod, H, hT, Y, QT, bufs, small = sb["mod"], sb["H"], sb["hT2"], sb["Y"], sb["QT2"], sb["bufs"], sb["small2"]
    used = [0]

    def sm(n):
        used[0] += n
        return small[:, used[0] - n:used[0]]

    par = st.count()
    crow, gains, qkg, sub, sink = sb["crow"], sb["gains"], sb["qkg"], sb["sub"], sb["sink"]
    act.dma(par, crow[:, 0, :], A["c_2"].rearrange("o (k p) -> (o k) p", p=P))
    act.dma(par, crow[:, 1, :], A["c_ctx_2"].rearrange("(k p) -> k p", p=P))
    for j, name in enumerate(("norm1_gain_2", "norm2_gain_2")):
        act.dma(par, gains[:, j, :], A[name][layer:layer + 1, :].to_broadcast([P, D]))
    for j, name in enumerate(("q_norm_gain_2", "k_norm_gain_2")):
        act.dma(par, qkg[:, j, :], A[name][layer:layer + 1, :].to_broadcast([P, HD2]))
    act.dma(par, sink[:, :], A["attn_sinks_2"][0:1, :].to_broadcast([P, H2]))
    have = act.dma(par, sub[:, 0:2, :], A["peer_sub_keys_2"][layer].rearrange("a k d -> k a d"))
    bias = Turns([(b, st.count()) for b in (sb["brow"][:, j, :] for j in range(3))])
    ws = Stream(st, sb["ring"], plan)

    i, ps, free = st.ps.take()
    t = pe.do(turned([(ps[:, 0, 8 * v:8 * v + 8], crow[:, v, :]) for v in range(2)]
                     + [(ps[:, 0, P * (a + 1):P * (a + 2)], sub[:, a, :]) for a in range(2)], ident), have, free)
    cT = sm(16)
    e = dve.do(cp(cT, ps[:, 0, 0:16]), t)
    have_sub = dve.do(cp(sub[:, 2:4, :].rearrange("p a n -> p (a n)"), ps[:, 0, P:3 * P]), t)
    st.ps.done(i, have_sub)
    sg = sm(16)
    t = sigmoid_of(st, sg, cT, e)
    have_c = dve.do(tt(cT, cT, sg, ALU.mult), t)
    c_of = cT.rearrange("p (v k) -> p v k", v=2)

    mrows = Turns([(sb["mrow"][:, j, :], st.count()) for j in range(2)])
    spill = st.count()
    spilled, kv_spilled = None, None

    def modulation(first, norm_gain, kinds, *after):
        nonlocal spilled
        if latents:
            for j in range(3):
                t = act.dma(par, mod[:, 0, j, :], kept["mod"][0:1, first // 2 + j, :].to_broadcast([P, D]), *after)
            made.append(dve.do(stt(mod[:, 0, 1, :], mod[:, 0, 1, :], 1.0, gains[:, norm_gain, :], ALU.add, ALU.mult), t, have))
            made.append(t)
            return
        for c in range(6):
            w, landed = ws.take()
            bi, (brow, count), bfree = bias.take()
            b = act.dma(count, brow, A["ada_b_2"][layer:layer + 1, (first + c) * 512:(first + c + 1) * 512].to_broadcast([2, 512]), bfree, *after)
            i, ps, free = st.ps.take()
            t = pe.do(mm_group([(ps[0:2, 0, :], [(c_of[:, :, k], w[:, k, :]) for k in range(KT)])]), landed, have_c, free)
            ws.done(t)
            mi, (mrow, kept_count), mfree = mrows.take()
            e = dve.do(tt(mrow, ps[0:2, 0, :], brow, ALU.add), t, b, mfree, *after)
            st.ps.done(i, e)
            bias.done(bi, e)
            i, ps, free = st.ps.take()
            t = pe.do(mm_group([(ps[:, v, :], [(sel[0:2, v, :], mrow)]) for v in kinds]), e, free)
            if context:
                spilled = act.dma(kept_count, kept["mod"][:, (first + c) // 2, (c % 2) * 512:(c % 2 + 1) * 512], mrow, e)
            mrows.done(mi, t, spilled)
            dst = mod[:, :, c // 2, (c % 2) * 512:(c % 2 + 1) * 512]
            if c // 2 == 1:
                for v in kinds:
                    e = dve.do(stt(dst[:, v, :], ps[:, v, :], 1.0, gains[:, norm_gain, (c % 2) * 512:(c % 2 + 1) * 512], ALU.add, ALU.mult), t, have, *after)
                made.append(e)
            else:
                e = act.do(af(dst[:, kinds[0]:kinds[-1] + 1, :], ps[:, kinds[0]:kinds[-1] + 1, :], ACT.Copy), t, *after)
                made.append(e)
            st.ps.done(i, e)

    def norm_modulate(tiles, *after):
        ss, rs = sm(4), sm(4)
        a = [act.do(af(H[:, g, :], xs[g], ACT.Square, acc=ss[:, j:j + 1]), *after) for j, g in enumerate(tiles)]
        n = len(tiles)
        r = rms_scale(st, rs[:, 0:n], ss[:, 0:n], D, n, C("m05")[:, 0:n], a)
        ready = []
        for j, g in enumerate(tiles):
            t = dve.do(stt(H[:, g, :], xs[g], rs[:, j:j + 1], mod[:, g // 2, 1, :], ALU.mult, ALU.mult), r, made)
            t = dve.do(tt(H[:, g, :], H[:, g, :], mod[:, g // 2, 0, :], ALU.add), t)
            ready.append(transpose_H(g, t))
        return ready

    def transpose_H(g, *after):
        i, ps, free = st.ps.take()
        t = pe.do(turned([(ps[:, k // 4, (k % 4) * P:(k % 4 + 1) * P], H[:, g, k * P:(k + 1) * P]) for k in range(KT)], ident), *after, free)
        t = act.do(af(hT[:, :, g * P:(g + 1) * P], flat(ps, "p b (k n) -> p (b k) n", k=4), ACT.Copy), t)
        st.ps.done(i, t)
        return t

    def project(w, landed, tiles, after):
        i, ps, free = st.ps.take()
        t = pe.do(mm_group([(ps[:, j, :], [(hT[:, k, g * P:(g + 1) * P], w[:, k, :]) for k in range(KT)])
                            for j, g in enumerate(tiles)]), landed, after, free)
        return i, ps, t

    made = []
    joined = None
    if latents:
        back = st.count()
        for src, dst in ((kept["xc"], sb["xc"][:, :, :]), (kept["PO"], H[:, 2:4, :])):
            act.dma(back, dst, src.rearrange("t p n -> p t n"))
        t = act.dma(back, mod[:, 1, 2, :], kept["mod"][1:2, 5, :].to_broadcast([P, D]))
        act.dma(back, QT[:, H2:H2 + KV2, 2 * P:4 * P], kept["kT"].rearrange("p (h n) -> p h n", h=KV2))
        have_kv = act.dma(back, Y[:, 2:4, (H2 + KV2) * HD2:(H2 + 2 * KV2) * HD2], kept["v"].rearrange("p (t n) -> p t n", t=2))
        for j in range(2):
            t = dve.do(tt(H[:, 2 + j, :], H[:, 2 + j, :], mod[:, 1, 2, :], ALU.mult), t, have_kv)
            joined = dve.do(tt(xs[2 + j], xs[2 + j], H[:, 2 + j, :], ALU.add), t)
    modulation(0, 0, [1] if context else [0, 1])
    rows_spilled = [(count.sem, count.n) for _, count in mrows.bufs if context]
    ready = norm_modulate(h_tiles)
    have_Y = []
    for c in range(3):
        w, landed = ws.take()
        for g in (0, 2):
            if g not in (q_tiles if c < 2 else h_tiles):
                continue
            i, ps, t = project(w, landed, (g, g + 1), ready)
            e = act.do(af(Y[:, g:g + 2, c * 512:(c + 1) * 512], ps[:, :, :], ACT.Copy), t)
            st.ps.done(i, e)
            have_Y.append(e)
        ws.done(t)

    rs = sm(40)
    nq = len(q_tiles)
    parts = [(0, H2, q_tiles, 0, rs[:, 0:8 * nq]), (H2, KV2, h_tiles, 1, rs[:, 32:32 + 2 * len(h_tiles)])]
    normed = []
    for h0, nh, tiles, gain, r in parts:
        for j, g in enumerate(tiles):
            y = Y[:, g, h0 * HD2:(h0 + nh) * HD2]
            scr = QT[:, :].rearrange("p h n -> p (h n)")[:, 0:nh * HD2]
            t = dve.do(tt(scr, y, y, ALU.mult), have_Y, normed, rows_spilled)
            t = dve.do(red(r[:, j * nh:(j + 1) * nh], scr.rearrange("p (h d) -> p h d", d=HD2), ALU.add), t)
            normed = [t]
        t = rms_scale(st, r, r, HD2, len(tiles) * nh, C("m05")[:, 0:len(tiles) * nh], t)
        if h0 == 0:
            t = dve.do(ts(r, r, HD2 ** -0.5, None, ALU.mult), t)
        for j, g in enumerate(tiles):
            y = Y[:, g, h0 * HD2:(h0 + nh) * HD2].rearrange("p (h d) -> p h d", d=HD2)
            a = dve.do(tt(y, y, wide(r[:, j * nh:(j + 1) * nh], [P, nh, HD2], 2), ALU.mult), t)
            a = dve.do(tt(y, y, qkg[:, gain:gain + 1, :].to_broadcast([P, nh, HD2]), ALU.mult), a, have)
            normed.append(a)
    tmp = bufs[:, 0:2560].rearrange("p (j h a d) -> p j h a d", j=4, h=10, a=2)
    u = None
    for g in (0, 1) if not context else ():
        y = Y[:, g, 0:10 * HD2].rearrange("p (h a b d) -> p h a b d", h=10, a=2, b=2)
        for a in range(2):
            y1, y2 = y[:, :, a, 0, :], y[:, :, a, 1, :]
            tab = lambda name: wide(C(name)[:, g * 64 + a * 32:g * 64 + a * 32 + 32], [P, 10, 32], 1)
            ta = [tmp[:, j, :, a, :] for j in range(4)]
            dve.do(tt(ta[0], y1, tab("cos2"), ALU.mult), normed, u)
            dve.do(tt(ta[1], y2, tab("sin2"), ALU.mult))
            dve.do(tt(ta[2], y1, tab("sin2"), ALU.mult))
            v = dve.do(tt(ta[3], y2, tab("cos2"), ALU.mult))
            dve.do(tt(y1, ta[0], ta[1], ALU.subtract), v)
            w_ = dve.do(tt(y2, ta[2], ta[3], ALU.add))
        u = w_
    have_QT = [have_kv] if latents else []
    for hp in range(5):
        tiles = q_tiles if hp < 4 else h_tiles
        cols = slice(tiles[0] * P, (tiles[-1] + 1) * P)
        i, ps, free = st.ps.take()
        t = pe.do(turned([(ps[:, j, g * P:(g + 1) * P], Y[:, g, (2 * hp + j) * HD2:(2 * hp + j + 1) * HD2]) for j in range(2) for g in tiles], ident),
                  u, normed, free)
        t = act.do(af(QT[:, 2 * hp:2 * hp + 2, cols], ps[:, :, cols], ACT.Copy), t, normed, rows_spilled)
        st.ps.done(i, t)
        have_QT.append(t)
    if context:
        act.dma(spill, kept["kT"].rearrange("p (h n) -> p h n", h=KV2), QT[:, H2:H2 + KV2, 2 * P:4 * P], t)
        kv_spilled = act.dma(spill, kept["v"].rearrange("p (t n) -> p t n", t=2), Y[:, 2:4, (H2 + KV2) * HD2:(H2 + 2 * KV2) * HD2], have_Y)

    pbufs = Turns([(bufs[:, 1536 * j:1536 * j + 512], bufs[:, 1536 * j + 512:1536 * j + 1024], bufs[:, 1536 * j + 1024:1536 * j + 1536], j) for j in range(2)]
                  + [(sb["bufs3"][:, 0:512], sb["bufs3"][:, 512:1024], sb["bufs3"][:, 1024:1536], 2)])
    pbufs.free = [[u], [u], []]
    stat = sm(12)
    done = {g: [] for g in q_tiles}

    def head(g, h):
        lo = 0 if g < 2 else 2 * P
        nk = 4 * P - lo
        bi, (sc, pr, pT, j), bfree = pbufs.take()
        mx, den, ex = (stat[:, 4 * j + a:4 * j + a + 1] for a in range(3))
        i, ps, free = st.ps.take()
        a = pe.do(mm_group([(ps[:, 0, 0:nk], [(QT[:, h, g * P:(g + 1) * P], QT[:, H2 + h // 4, lo:4 * P])])]), have_QT, free)
        src = ps[:, 0, 0:nk]
        if last:
            a = dve.do(tt(sc, src, C("win")[:, g * 512:(g + 1) * 512], ALU.add), a, bfree)
            st.ps.done(i, a)
            src = sc
        a = dve.do(red(mx, src, ALU.max, negate=True), a, bfree)
        if last:
            a = dve.do(stt(mx, sink[:, h:h + 1], -1.0, mx, ALU.mult, ALU.min), a, have)
        b = act.do(af(pr[:, 0:nk], src, ACT.Exp, bias=mx, acc=den), a, bfree)
        if not last:
            st.ps.done(i, b)
        yield
        if last:
            s_ = act.do(af(ex, sink[:, h:h + 1], ACT.Exp, bias=mx), a)
            b2 = dve.do(tt(den, den, ex, ALU.add), b, s_)
        else:
            b2 = b
        r = dve.do(lambda e: e.reciprocal(den, den), b2)
        i, ps, free = st.ps.take()
        c = pe.do(turned([(ps[:, 0, k * P:(k + 1) * P], pr[:, k * P:(k + 1) * P]) for k in range(nk // P)], ident), b, free)
        c = (act if h % 2 else dve).do((af(pT[:, 0:nk], ps[:, 0, 0:nk], ACT.Copy) if h % 2 else cp(pT[:, 0:nk], ps[:, 0, 0:nk])), c, bfree)
        st.ps.done(i, c)
        yield
        i, ps, free = st.ps.take()
        d = pe.do(mm_group([(ps[:, 0, 0:HD2], [(pT[:, k * P:(k + 1) * P], Y[:, k + lo // P, (H2 + KV2 + h // 4) * HD2:(H2 + KV2 + h // 4 + 1) * HD2])
                                               for k in range(nk // P)])]), c, free)
        e = dve.do(ts(H[:, g, h * HD2:(h + 1) * HD2], ps[:, 0, 0:HD2], den, None, ALU.mult), d, r, ready)
        st.ps.done(i, e)
        pbufs.done(bi, e)
        done[g].append(e)
        yield

    in_turn([head(g, h) for g in q_tiles for h in range(H2)], 3)
    ready = [transpose_H(g, done[g]) for g in q_tiles]

    prod = Turns([bufs[:, 0:1024].rearrange("p (t n) -> p t n", t=2), bufs[:, 1024:2048].rearrange("p (t n) -> p t n", t=2)])
    all_done = [x_ for g in q_tiles for x_ in done[g]]
    prod.free = [all_done, all_done]
    res = []
    for c in range(2):
        w, landed = ws.take()
        for g in q_tiles[::2]:
            i, ps, t = project(w, landed, (g, g + 1), ready)
            bi, buf, bfree = prod.take()
            gate = mod[:, g // 2, 2:3, c * 512:(c + 1) * 512].to_broadcast([P, 2, 512])
            e = dve.do(tt(buf, ps[:, :, :], gate, ALU.mult), t, made, bfree)
            st.ps.done(i, e)
            for j in range(2):
                xv = xs[g + j][:, c * 512:(c + 1) * 512]
                e = dve.do(tt(xv, xv, buf[:, j, :], ALU.add), e)
            prod.done(bi, e)
            res.append(e)
        ws.done(t)

    made = []
    modulation(6, 1, [1] if context else [0], res, joined)
    ready = norm_modulate(q_tiles, res)
    SC = sb["SC"]
    n, first = len(q_tiles) * P, q_tiles[0]
    qb = Turns([sb["bufs3"][:, 0:512], sb["bufs3"][:, 512:1024], sb["bufs3"][:, 1024:1536]])
    qb.free = [all_done] * 3
    for c in range(4):
        w, landed = ws.take()
        for b in range(4):
            blk = 4 * c + b
            i, ps, free = st.ps.take()
            t = pe.do(mm_group([(ps[:, 0, 0:n], [(w[:, k, b * P:(b + 1) * P], hT[:, k, first * P:first * P + n]) for k in range(KT)])]), landed, ready, free)
            bi, buf, bfree = qb.take()
            e = act.do(af(buf[:, 0:n], ps[:, 0, 0:n], ACT.Copy), t, bfree)
            s_ = pe.do(mm_group([(ps[:, 1, j * P:(j + 1) * P], [(buf[:, j * P:(j + 1) * P], sub[:, 2 + blk % 2, :])]) for j in range(len(q_tiles))]), e, have_sub)
            qb.done(bi, s_)
            f = dve.do(cp(SC[:, :, :].rearrange("p (g h) n -> p g h n", h=PH)[:, :, blk // 2, (blk % 2) * P:(blk % 2 + 1) * P],
                          ps[:, 1, 0:n].rearrange("p (g n) -> p g n", n=P)), s_, have_QT, all_done, kv_spilled)
            st.ps.done(i, e, f)
        ws.done(t)
    if not context:
        dve.do(lambda e: e.memset(sb["PO"][:, :, :], 0.0), all_done)
        return
    mods_spilled = [(count.sem, count.n) for _, count in mrows.bufs]
    for name, src in (("H", H[:, 2:4, :]), ("xc", sb["xc"][:, :, :]), ("SC", SC[:, :, :].rearrange("p (g h) n -> p g (h n)", h=PH))):
        t = sp.dma(spill, kept[name].rearrange("t p n -> p t n"), src, f, ready, res)
    sp.do(lambda e: e.nop(), t, mods_spilled)


def routing(*arguments):
    steps = routing_steps(*arguments)
    while True:
        try:
            next(steps)
        except StopIteration as end:
            return end.value


def routing_steps(queue, rt, C, scores, after, idx, g):
    dve, act = queue.dve, queue.act
    v, ix, cand, cand2, tv, tp, abu, abf, ixf, eq, pick = (rt[n] for n in ("v", "ix", "cand", "cand2", "tv", "tp", "abu", "abf", "ixf", "eq", "pick"))

    def top16(vals, idxs, a, b, t):
        x = dve.do(lambda e: e.max(vals[:, 0:8], a), t)
        yield
        dve.do(lambda e: e.max_index(idxs[:, 0:8], vals[:, 0:8], a), x)
        yield
        x = dve.do(lambda e: e.match_replace(b, vals[:, 0:8], a, -3.0e38), x)
        yield
        x = dve.do(lambda e: e.max(vals[:, 8:16], b), x)
        yield
        return dve.do(lambda e: e.max_index(idxs[:, 8:16], vals[:, 8:16], b), x)

    t = after
    for half in range(2):
        t = yield from top16(v[:, half, :], ix[:, half, :], scores[:, half * NK:(half + 1) * NK], cand2[:, 0:NK], t)
    copied = t
    sums = cand[:, :].rearrange("p (a b) -> p a b", a=TOPK)
    t = dve.do(tt(sums, wide(v[:, 0, :], [P, TOPK, TOPK], 2), wide(v[:, 1, :], [P, TOPK, TOPK], 1), ALU.add), t)
    yield
    t = yield from top16(tv, tp, cand, cand2, t)
    yield
    m = dve.do(ts(rt["nm"], tv[:, 0:1], -1.0, None, ALU.mult), t)
    ex = act.do(af(rt["ex"], tv, ACT.Exp, bias=rt["nm"], acc=rt["z"]), m)
    dve.do(lambda e: e.tensor_scalar(abu[:, 0, :], tp, 4, None, ALU.logical_shift_right), t)
    t = dve.do(lambda e: e.tensor_scalar(abu[:, 1, :], tp, TOPK - 1, None, ALU.bitwise_and), t)
    yield
    t = dve.do(cp(abf, abu), t)
    t2 = dve.do(cp(ixf, ix), copied)
    iota = C("iota")
    for half in range(2):
        q = dve.do(tt(eq[:, half], wide(abf[:, half, :], [P, TOPK, TOPK], 2), wide(iota, [P, TOPK, TOPK], 1), ALU.is_equal), t)
        yield
        q = dve.do(tt(eq[:, half], eq[:, half], wide(ixf[:, half, :], [P, TOPK, TOPK], 1), ALU.mult), q, t2)
    t = dve.do(red(pick.rearrange("p a k -> p (a k)"), eq.rearrange("p a k j -> p (a k) j"), ALU.add), q)
    made = dve.do(stt(idx, pick[:, 0, :], float(NK), pick[:, 1, :], ALU.mult, ALU.add), t)
    yield
    r = dve.do(lambda e: e.reciprocal(rt["z"], rt["z"]), ex)
    dve.do(ts(g, rt["ex"], rt["z"], None, ALU.mult), r)
    return made


ALL = 1 << 20


class LoopLane(Lane):

    def waits(self, after):
        flatten, todo = [], list(after)
        while todo:
            a = todo.pop(0)
            if isinstance(a, list):
                todo = a + todo
            elif a is not None:
                flatten.append(a)
        best = {}
        for a in flatten:
            key = (id(a[0]), len(a) == 3)
            if self.seen.get(key, 0) < a[1] and (key not in best or best[key][1] < a[1]):
                best[key] = a
        now = {key[0] for key in [*self.seen, *best] if not key[1]}
        best = {key: a for key, a in best.items() if not (key[1] and key[0] in now)}
        for key, a in best.items():
            self.seen[key] = a[1]
        return list(best.values())

    def play_turn(self, e, f, per_turn, go):
        for fn, waits, sem, by in self.steps:
            values = [e.to_reg(f * per_turn[id(w[0])][0] + min(w[1], per_turn[id(w[0])][0])
                             + (per_turn[id(w[0])][1] if len(w) == 2 else 0)) for w in waits]
            if waits:
                e.wait_ge(go, 1)
            for w, v in zip(waits, values):
                e.wait_ge(w[0], v)
            fn(e).then_inc(sem, by)


def weights(st, rt, g, *after):
    dve, act = st.dve, st.act
    dots, w, z1, z2 = rt["dots"], rt["w"], rt["z1"], rt["z2"]
    t = dve.do(tt(z1, dots, dots, ALU.mult), *after)
    t = dve.do(ts(z1, z1, GELU_C * 0.044715, GELU_C, ALU.mult, ALU.add), t)
    t = dve.do(tt(z1, z1, dots, ALU.mult), t)
    t = dve.do(ts(z1, z1, -EXP_MAX, None, ALU.max), t)
    t = act.do(af(z2, z1, ACT.Exp, scale=-1.0), t)
    t = dve.do(ts(z2, z2, 1.0, None, ALU.add), t)
    t = dve.do(lambda e: e.reciprocal(z2, z2), t)
    t = dve.do(tt(w, dots, z2, ALU.mult), t)
    return dve.do(tt(w, w, g, ALU.mult), t)


def gather_row(ring_slot, tab, idx, k, layer):
    return lambda e: e.indirect_dma_start(out=ring_slot, out_offset=None, in_=tab,
                                          in_offset=bass.IndirectOffsetOnAxis(ap=idx[:, k:k + 1], axis=0),
                                          element_offset=layer * NE * D)


def dot_with(slot, h, out):
    return lambda e: e.scalar_tensor_tensor(out=slot, in0=slot, scalar=1.0, in1=h(), op0=ALU.mult, op1=ALU.mult, accum_out=out)


def context_experts(st, ex, A, C, kept, l):
    dve, act, pool, sp, rt = st.dve, st.act, st.pool, st.sp, ex["rt"]
    H, PO, SC = ex["H"], ex["PO"], ex["SC"].rearrange("p (h n) -> p h n", h=PH)
    u_tab, v_tab = (A[n].rearrange("l e d -> (l e) d") for n in ("peer_u_2", "peer_v_2"))
    slots = Turns([(ring, st.count()) for ring in ex["ring"]])
    st.soft += [c for _, c in slots.bufs]
    par = st.count()
    at = lambda name: kept[name][bass.DynSlice(l, 1)].rearrange("o p n -> (o p) n")
    act.dma(par, H, at("H"))
    have = act.dma(par, SC, at("SC"))
    cleared = dve.do(lambda e: e.memset(PO, 0.0))
    idx, g = (lambda f: rt["idx"][:, f % 3, :]), (lambda f: rt["g"][:, f % 3, :])
    routed, weighed, added = {}, {}, [cleared]
    waiting = []

    def gather(tab, f, k, use):
        i, (buf, count), free = slots.take()
        count.n += 16
        pool.steps.append((gather_row(buf, tab, idx(f), k, 0), pool.waits([routed[f], free]), count.sem, 16))
        landed = (count.sem, count.n)
        waiting.append(lambda: slots.done(i, use(buf, k, landed)))
        while len(waiting) > len(slots.bufs) - 3:
            waiting.pop(0)()

    def dot(buf, k, landed):
        return dve.do(dot_with(buf, lambda: H, rt["dots"][:, k:k + 1]), landed, have)

    def add(f):
        def fn(buf, k, landed):
            added[0] = dve.do(stt(PO, buf, rt["w"][:, k:k + 1], PO, ALU.mult, ALU.add), landed, weighed[f], added[0])
            return added[0]
        return fn

    def weigh(f):
        weighed[f] = weights(st, rt, g(f), (dve.sem, dve.n))

    for f in range(2):
        routed[f] = yield from routing_steps(st, rt, C, SC[:, f, :], have, idx(f), g(f))
    for k in range(TOPK):
        gather(u_tab, 0, k, dot)
        yield
    waiting.append(lambda: weigh(0))
    for f in range(PH):
        steps = routing_steps(st, rt, C, SC[:, f + 2, :], have, idx(f + 2), g(f + 2)) if f + 2 < PH else iter(())
        for k in range(TOPK):
            if f + 1 < PH:
                gather(u_tab, f + 1, k, dot)
                yield
            gather(v_tab, f, k, add(f))
            for _ in range(3 if TOPK // 2 <= k < TOPK - 1 else 1 << 10 if k == TOPK - 1 else 0):
                try:
                    next(steps)
                except StopIteration as end:
                    if end.value is not None:
                        routed[f + 2] = end.value
                    break
            yield
        if f + 1 < PH:
            waiting.append(lambda f=f: weigh(f + 1))
    for use in waiting:
        use()
    out = st.count()
    t = sp.dma(out, at("PO"), PO, (dve.sem, dve.n))
    sp.do(lambda e: e.nop(), t)


def first_head(st, sb, A, C, layer):
    rt, ring, SC = sb["rt"], sb["gring"], sb["SC"]
    u_tab = A["peer_u_2"].rearrange("l e d -> (l e) d")
    made = routing(st, rt, C, SC[:, 0, :], None, rt["idx"][:, 0, :], rt["g"][:, 0, :])
    for k in range(TOPK):
        c = st.count()
        c.n = 16
        st.soft.append(c)
        st.pool.steps.append((gather_row(ring[:, k, :], u_tab, rt["idx"][:, 0, :], k, layer), st.pool.waits([made]), c.sem, 16))
    last = (st.dve.sem, st.dve.n)
    st.dve.do(lambda e: e.memset(sb["psum"][:, 0:2, :], 0.0))
    routing(st, rt, C, SC[:, 1, :], last, rt["idx"][:, 1, :], rt["g"][:, 1, :])
    for k in range(TOPK):
        st.dve.do(dot_with(ring[:, k, :], lambda: sb["H"][:, 0, :], rt["dots"][:, k:k + 1]), (st.soft[k].sem, 16))


def experts(nc, st, sb, A, C, layer, tiles):
    rt, ring, H, PO, SC = sb["rt"], sb["gring"], sb["H"], sb["PO"], sb["SC"]
    u_tab, v_tab = (A[n].rearrange("l e d -> (l e) d") for n in ("peer_u_2", "peer_v_2"))
    st.dve, st.act, st.pe, st.pool = (LoopLane(x.sem) for x in (st.dve, st.act, st.pe, st.pool))
    dve, act, pe, pool = st.dve, st.act, st.pe, st.pool
    go = st.sem()
    NS = TOPK // 2
    u_slot, v_slot = [ring[:, j, :] for j in range(NS)], [ring[:, NS + j, :] for j in range(NS)]
    u_in, v_in = [st.count() for _ in range(NS)], [st.count() for _ in range(NS)]
    acc = sb["psum"][:, 0:2, :]
    cur = {}
    at_tile = lambda buf, g: buf[:, bass.DynSlice(cur[g], 1), :].rearrange("p o n -> p (o n)")
    as_acc = lambda ap: ap.rearrange("p (b n) -> p b n", b=2)

    def add(k):
        def fn(e):
            for half in range(2):
                last = e.matmul(acc[:, half, :], rt["diag"][:, k, :], v_slot[k % NS][:, half * 512:(half + 1) * 512],
                                start=(k == 0), stop=(k == TOPK - 1))
            return last
        return fn

    size = {}
    for part in range(2):
        start = {id(x): x.n for x in (dve, act, pe, pool)}
        here = lambda lane, n: (lane.sem, start[id(lane)] + n)
        if part == 0:
            before = lambda lane, n: (lane.sem, ALL, "before") if n is None else (lane.sem, size[id(lane)] + n, "before")
            size[id(pe)] = TOPK
        else:
            before = lambda lane, n: (lane.sem, size[id(lane)] if n is None else n)
        idx, g, v_idx = rt["idx"][:, part, :], rt["g"][:, part, :], rt["v_idx"][:, part, :]
        next_idx = rt["idx"][:, 1 - part, :]
        kept = dve.do(cp(v_idx, idx), before(dve, None))
        t = weights(st, rt, g, before(dve, None))
        have_w = dve.do(tt(rt["diag"], wide(C("ident"), [P, TOPK, P], 1), wide(rt["w"], [P, TOPK, P], 2), ALU.mult), t, before(pe, TOPK))
        tile = "g_before" if part == 0 else "g"
        taken = dve.do((lambda q: lambda e: e.tensor_tensor(as_acc(at_tile(PO, q)), as_acc(at_tile(PO, q)), acc, ALU.add))(tile), before(pe, TOPK))
        staged = act.do((lambda q: lambda e: e.copy(rt["scores"], SC[:, bass.DynSlice(cur[q], 1), :].rearrange("p o n -> p (o n)")))(f"f_routed{part}"),
                        before(dve, None))
        made = routing(st, rt, C, rt["scores"], staged, idx, g)
        route_step = made[1] - start[id(dve)]
        dot0 = dve.n - start[id(dve)]
        tile = "g" if part == 0 else "g_after"
        for k in range(TOPK):
            dve.do(dot_with(u_slot[k % NS], (lambda q: lambda: at_tile(H, q))(tile), rt["dots"][:, k:k + 1]),
                   have_w, (u_in[k % NS].sem, 32 * part + 16 * (k // NS) + 16))
        size[id(dve)], size[id(act)] = dve.n - start[id(dve)], act.n - start[id(act)]
        for k in range(TOPK):
            pe.do(add(k), have_w, taken, (v_in[k % NS].sem, 32 * part + 16 * (k // NS) + 16))
        for k in range(TOPK):
            dotted = before(dve, dot0 + k + NS + 1) if k < NS else here(dve, dot0 + k - NS + 1)
            added = before(pe, k + NS + 1) if k < NS else here(pe, k - NS + 1)
            for fn, count, after in (
                (gather_row(u_slot[k % NS], u_tab, next_idx, k, layer), u_in[k % NS], [before(dve, route_step), dotted]),
                (gather_row(v_slot[k % NS], v_tab, v_idx, k, layer), v_in[k % NS], [kept, added]),
            ):
                count.n += 16
                pool.steps.append((fn, pool.waits(after), count.sem, 16))
    per_turn = {id(x.sem): (x.n, x.n) for x in (dve, act, pe, pool)}
    per_turn |= {id(s.sem): (s.n, 0) for s in u_in + v_in}

    def play(lane):
        def fn(e):
            if lane.n:
                e.sem_inc(lane.sem, lane.n)
            e.sem_inc(go, 1)
            with e.Fori(0, tiles) as g:
                with e.Fori(0, PH // 2) as pair:
                    turn = g * (PH // 2) + pair
                    cur["g"], cur["g_before"] = g, ((turn + 4 * tiles - 1) >> 2) & (tiles - 1)
                    cur["g_after"] = ((turn + 1) >> 2) & (tiles - 1)
                    cur["f_routed0"], cur["f_routed1"] = ((turn * 2 + 2 + q) & (tiles * PH - 1) for q in range(2))
                    lane.play_turn(e, turn, per_turn, go)
            if lane is dve:
                total = per_turn[id(pe.sem)][0] * (tiles * PH // 2 + 1)
                e.wait_ge(pe.sem, total)
                e.wait_ge(dve.sem, per_turn[id(dve.sem)][0] * (tiles * PH // 2 + 1))
                e.tensor_tensor(as_acc(PO[:, tiles - 1, :]), as_acc(PO[:, tiles - 1, :]), acc, ALU.add).then_inc(dve.sem, 1)
            if lane is pool:
                for s in u_in + v_in:
                    e.wait_ge(s.sem, s.n * tiles * (PH // 2))
                e.dma_reset()
        return fn
    with nc.Block() as block:
        block.scalar(play(act))
        block.vector(play(dve))
        block.gpsimd(play(pool))
        block.tensor(play(pe))
    nc.all_engine_barrier(sems_to_clear=range(st.sems[0].num, st.sems[st.used - 1].num + 1))


ROUTE = (("v", 32), ("ix", 32), ("cand", 256), ("cand2", 256), ("tv", 16), ("tp", 16), ("abu", 32), ("abf", 32), ("ixf", 32), ("eq", 512), ("pick", 32),
         ("nm", 1), ("z", 1), ("ex", 16), ("idx", 48), ("g", 48), ("dots", 16), ("w", 16), ("z1", 16), ("z2", 16))
ROUTE_COLS = sum(n for _, n in ROUTE)
GATHERS_PER_US = 0.75


def routing_buffers(buf):
    rt, at = {}, 0
    for name, n in ROUTE:
        rt[name] = buf[:, at:at + n]
        at += n
    for name in ("v", "ix", "abu", "abf", "ixf", "pick", "idx", "g"):
        rt[name] = rt[name].rearrange("p (a k) -> p a k", k=TOPK)
    rt["eq"] = rt["eq"].rearrange("p (a k j) -> p a k j", a=2, j=TOPK)
    for name in ("ix", "tp", "abu", "idx"):
        rt[name] = rt[name].bitcast(U32)
    return rt


def second_block_memory(mem, x, psum):
    sb = {"psum": psum}
    for name, shape in (("mod", [P, 2, 3, D]), ("H", [P, 4, D]), ("gring", [P, TOPK, D]), ("scores", [P, 11264]),
                        ("work", [P, 4608]), ("xc", [P, NT, D]), ("small2", [P, 128]), ("gains", [P, 2, D]),
                        ("crow", [8, 2, P]), ("qkg", [P, 2, HD2]), ("sub", [P, 4, P]), ("sink", [P, H2])):
        sb[name] = mem(name, shape)
    gflat = flat(sb["gring"][:, :, :], "p k n -> p (k n)")
    sb["ring"] = [gflat[:, 4096 * i:4096 * (i + 1)] for i in range(3)]
    sb["hT2"] = gflat[:, 12288:16384].rearrange("p (k n) -> p k n", k=KT)
    big, work = sb["scores"], sb["work"]
    sb["Y"] = big[:, 0:6144].rearrange("p (g n) -> p g n", g=4)
    sb["QT2"] = big[:, 6144:11264].rearrange("p (h n) -> p h n", h=10)
    at = NT * PH * 2 * NK
    sb["SC"] = big[:, 0:at].rearrange("p (f n) -> p f n", n=2 * NK)
    routes = big[:, at:at + ROUTE_COLS + 2 * NK + 2 * TOPK]
    at = 11264 - 2560
    sb["brow"] = big[0:2, at:at + 1536].rearrange("p (j n) -> p j n", j=3)
    sb["mrow"] = big[0:2, at + 1536:at + 2560].rearrange("p (j n) -> p j n", j=2)
    sb["bufs"], sb["bufs3"] = work[:, 0:3072], work[:, 3072:4608]
    sb["PO"] = work[:, 0:2 * D].rearrange("p (g n) -> p g n", g=NT)
    rt = routing_buffers(routes)
    rt["diag"] = flat(sb["gains"][:, :, :], "p a n -> p (a n)").rearrange("p (k n) -> p k n", k=TOPK)
    rt["scores"] = routes[:, ROUTE_COLS:ROUTE_COLS + 2 * NK]
    rt["v_idx"] = routes[:, ROUTE_COLS + 2 * NK:].rearrange("p (a k) -> p a k", a=2).bitcast(U32)
    sb["rt"] = rt
    return sb, [x[:, 0, :], x[:, 1, :], sb["xc"][:, 0, :], sb["xc"][:, 1, :]]


def build(nc, A, out, upto=99):
    with ExitStack() as ctx:
        mem = Memory(nc, ctx)
        sems = [ctx.enter_context(nc.semaphore(f"count{i}")) for i in range(44)]
        psum = ctx.enter_context(nc.psum_tensor("psum", [P, 8, 512], F32))
        consts = mem("consts", [P, CONSTS.shape[1]])
        C = lambda name: consts[:, CONST_COLS[name][0]:CONST_COLS[name][0] + CONST_COLS[name][1]]
        x = mem("x", [P, NT, D])

        st = Stage(nc, sems, psum)
        c = st.count()
        st.sp.dma(c, consts[:, :], A["consts"])
        t = st.sp.dma(c, x[:, :, :], A["x"].rearrange("o (t p) d -> p (o t) d", p=P))
        st.sp.do(lambda e: e.nop(), t)
        st.run()

        kept = {name: nc.dram_tensor(f"kept_{name}", shape, F32).ap() for name, shape in (
            ("mod", (2, N_MOD, D)), ("kT", (P, KV2 * S)), ("v", (P, 2 * KV2 * HD2)), ("H", (2, P, D)), ("xc", (2, P, D)),
            ("SC", (2, P, PH * 2 * NK)), ("PO", (2, P, D)))}
        with ExitStack() as block_memory:
            sb, xs = second_block_memory(Memory(nc, block_memory, "c_"), x, psum)
            st = Stage(nc, sems, psum)
            c = st.count()
            t = st.sp.dma(c, sb["xc"][:, :, :], A["ctx_2"].rearrange("o (t p) d -> p (o t) d", p=P))
            st.sp.do(lambda e: e.nop(), t)
            st.run()
            st = Stage(nc, sems, psum)
            attention_block(st, sb, A, C, xs, kept, 0, "context")
            st.run()

        with ExitStack() as block_memory:
            m1 = Memory(nc, block_memory)
            sb = {}
            for name, shape in (("hn", [P, NT, D]), ("hT", [P, KT, S]), ("arena", [P, 8192]), ("N", [P, NT, NAT]), ("sq", [P, NT * NG * HD]),
                                ("attn", [P, 6144]), ("small", [P, 640]), ("pe_rows", [32, P]), ("g6", [P, 6, HD]),
                                ("cw2", [P, 2, HD]), ("cols", [P, KT, 8]), ("kv", [16, 4 * HD])):
                sb[name] = m1(name, shape)
            ring = [m1(f"ring{i}", [P, 4096]) for i in range(2)]
            ex = {name: m1(f"ex_{name}", [P, n])[:, :] for name, n in (("H", D), ("PO", D), ("SC", PH * 2 * NK))}
            ex["ring"] = [m1(f"ex_ring{i}", [P, D])[:, :] for i in range(8)]
            ex["rt"] = routing_buffers(m1("ex_route", [P, ROUTE_COLS]))
            with nc.Fori(0, DEPTH) as l:
                st = Stage(nc, sems, psum)
                st.pe.beside, st.pe.rate = context_experts(st, ex, A, C, kept, l), GATHERS_PER_US
                first_block(st, sb, A, C, x, ring, l)
                for _ in st.pe.beside or ():
                    pass
                st.run()

        if upto == 1:
            st = Stage(nc, sems, psum)
            c = st.count()
            t = st.sp.dma(c, out.rearrange("o (t p) d -> p (o t) d", p=P), x[:, :, :])
            st.sp.do(lambda e: e.nop(), t)
            st.run()
            return

        with ExitStack() as block_memory:
            sb, xs = second_block_memory(Memory(nc, block_memory, "l_"), x, psum)
            for layer in range(DEPTH):
                st = Stage(nc, sems, psum)
                attention_block(st, sb, A, C, xs, kept, layer, "last" if layer == DEPTH - 1 else "latents")
                st.run()
                if upto == 2 + 2 * layer:
                    break
                st = Stage(nc, sems, psum)
                first_head(st, sb, A, C, layer)
                st.run()
                experts(nc, Stage(nc, sems, psum), sb, A, C, layer, NT)
                st = Stage(nc, sems, psum)
                for g in range(NT):
                    t = st.dve.do(tt(sb["PO"][:, g, :], sb["PO"][:, g, :], sb["mod"][:, 0, 2, :], ALU.mult))
                    t = st.dve.do(tt(xs[g], xs[g], sb["PO"][:, g, :], ALU.add), t)
                st.run()
                if upto == 3 + 2 * layer:
                    break

            st = Stage(nc, sems, psum)
            c = st.count()
            t = st.sp.dma(c, out.rearrange("o (t p) d -> p (o t) d", p=P), x[:, :, :])
            if upto < 99:
                t = st.sp.dma(c, A["dbg"].rearrange("(t p) d -> p t d", p=P), sb["xc"][:, :, :])
            st.sp.do(lambda e: e.nop(), t)
            st.run()


INPUTS = ["x", "w_in", "b_if", "conv_qk", "m_norm", "moba_qk_norm", "nsa_q_norm", "nsa_k_norm", "cmp_pe", "cmp_w1", "cmp_w2", "w_out",
          "norm_mix", "norm_ffn", "w_ff1", "w_ff2", "c_2", "ctx_2", "c_ctx_2", "ada_w_2", "ada_b_2", "norm1_gain_2", "norm2_gain_2",
          "w_qkv_2", "q_norm_gain_2", "k_norm_gain_2", "w_o_2", "attn_sinks_2", "peer_w_q_2", "peer_sub_keys_2", "peer_u_2", "peer_v_2"]


def kernel(**inputs):
    import concourse.bacc as bacc
    from concourse.bass_utils import run_bass_kernel_spmd

    nc = bacc.Bacc("TRN2", target_bir_lowering=False, num_devices=1)
    arrays = {name: np.ascontiguousarray(inputs[name]) for name in INPUTS}
    arrays["consts"] = CONSTS
    A = {name: nc.dram_tensor(f"in_{name}", a.shape, F32, kind="ExternalInput").ap() for name, a in arrays.items()}
    out = nc.dram_tensor("out", (1, S, D), F32, kind="ExternalOutput").ap()
    build(nc, A, out)
    r = run_bass_kernel_spmd(nc, [{f"in_{name}": a for name, a in arrays.items()}], core_ids=[0])
    return r.results[0]["out"]
```
